# Optimizing a Trainium2 kernel written in Bass

```python
import math
import jax, jax.numpy as jnp
from jax import lax
import numpy as np

D_MODEL = 1024
BATCH = 1
SEQ = 256
DEPTH = 2

MEM_LEN = 256
EPS = 1e-6
ROPE_THETA = 10000.0
A_HEADS = D_MODEL // 128
A_HEAD_DIM = 64
A_WIDTH = A_HEADS * A_HEAD_DIM
MOBA_BLOCK = 256
MOBA_TOPK = 3
MOBA_QCHUNK = 32
B_HEADS = D_MODEL // 128
B_NOPE = 64
B_ROPE = 32
B_VDIM = 64
B_Q_LORA = 3 * D_MODEL // 8
B_KV_LORA = D_MODEL // 4
B_WIDTH = B_HEADS * B_VDIM
ATTN_QBLOCK = 128
X_HEADS = 4
X_HEAD_DIM = 128
X_WIDTH = X_HEADS * X_HEAD_DIM
D_FF = ((8 * D_MODEL // 3 + 255) // 256) * 256
IN_WIDTH = 3 * A_WIDTH + B_Q_LORA + B_KV_LORA + B_ROPE + 2 * D_MODEL

kernel_name = "hybrid_moba_mla_gated_trunk"

F32 = jnp.float32

def rmsnorm(t, g):
    tf = t.astype(F32)
    y = tf * lax.rsqrt(jnp.mean(tf * tf, axis=-1, keepdims=True) + EPS)
    return (y * g.astype(F32)).astype(t.dtype)

def rope(t, pos):
    dim = t.shape[-1]
    half = dim // 2
    inv = jnp.exp(-math.log(ROPE_THETA) * (2.0 / dim) * jnp.arange(half, dtype=F32))
    ang = pos.astype(F32)[:, None, :, None] * inv
    cos, sin = jnp.cos(ang), jnp.sin(ang)
    tf = t.astype(F32)
    t1, t2 = tf[..., :half], tf[..., half:]
    return jnp.concatenate([t1 * cos - t2 * sin, t2 * cos + t1 * sin], axis=-1).astype(t.dtype)

def _heads(t, n):
    b, s, _ = t.shape
    return t.reshape(b, s, n, -1).transpose(0, 2, 1, 3)

def _merge(o):
    b, h, s, d = o.shape
    return o.transpose(0, 2, 1, 3).reshape(b, s, h * d)

def moba_attention(q, k, v):
    b, h, s, d = q.shape
    nb = -(-s // MOBA_BLOCK)
    pad = nb * MOBA_BLOCK - s
    kp = jnp.pad(k, ((0, 0), (0, 0), (0, pad), (0, 0)))
    vp = jnp.pad(v, ((0, 0), (0, 0), (0, pad), (0, 0)))
    kb = kp.reshape(b, h, nb, MOBA_BLOCK, d)
    vb = vp.reshape(b, h, nb, MOBA_BLOCK, d)
    kbar = jnp.mean(kb.astype(F32), axis=3)
    n_sel = min(MOBA_TOPK, nb)
    scale = d ** -0.5
    bi = jnp.arange(b)[:, None, None, None]
    hi = jnp.arange(h)[None, :, None, None]
    blk_ids = jnp.arange(nb)
    slot_ids = jnp.arange(n_sel)
    own_offsets = jnp.arange(MOBA_BLOCK)

    def chunk(c):
        start = c * MOBA_QCHUNK
        qc = lax.dynamic_slice_in_dim(q, start, MOBA_QCHUNK, axis=2)
        tq = start + jnp.arange(MOBA_QCHUNK)
        cur = start // MOBA_BLOCK
        gate = jnp.einsum('bhcd,bhnd->bhcn', qc.astype(F32), kbar)
        gate = jnp.where(blk_ids < cur, gate, -jnp.inf)
        _, sel = lax.top_k(gate, n_sel)
        ks = kb[bi, hi, sel]
        vs = vb[bi, hi, sel]
        s_sel = jnp.einsum('bhcd,bhcnkd->bhcnk', qc, ks, preferred_element_type=F32) * scale
        s_sel = jnp.where((slot_ids < cur)[:, None], s_sel, -jnp.inf)
        s_sel = s_sel.reshape(b, h, MOBA_QCHUNK, n_sel * MOBA_BLOCK)
        k_own = lax.dynamic_slice_in_dim(kp, cur * MOBA_BLOCK, MOBA_BLOCK, axis=2)
        v_own = lax.dynamic_slice_in_dim(vp, cur * MOBA_BLOCK, MOBA_BLOCK, axis=2)
        kpos = cur * MOBA_BLOCK + own_offsets
        s_own = jnp.einsum('bhcd,bhkd->bhck', qc, k_own, preferred_element_type=F32) * scale
        s_own = jnp.where(kpos[None, :] <= tq[:, None], s_own, -jnp.inf)
        p = jax.nn.softmax(jnp.concatenate([s_sel, s_own], axis=-1), axis=-1)
        p_sel = p[..., :n_sel * MOBA_BLOCK].reshape(b, h, MOBA_QCHUNK, n_sel, MOBA_BLOCK).astype(v.dtype)
        p_own = p[..., n_sel * MOBA_BLOCK:].astype(v.dtype)
        return (jnp.einsum('bhcnk,bhcnkd->bhcd', p_sel, vs)
                + jnp.einsum('bhck,bhkd->bhcd', p_own, v_own))

    out = lax.map(chunk, jnp.arange(s // MOBA_QCHUNK))
    return out.transpose(1, 2, 0, 3, 4).reshape(b, h, s, d)

def mla_attention(q_nope, q_pe, k_nope, k_pe, v):
    b, h, s, _ = q_nope.shape
    scale = (B_NOPE + B_ROPE) ** -0.5
    kpos = jnp.arange(s)

    def blk(i):
        st = i * ATTN_QBLOCK
        qn = lax.dynamic_slice_in_dim(q_nope, st, ATTN_QBLOCK, axis=2)
        qr = lax.dynamic_slice_in_dim(q_pe, st, ATTN_QBLOCK, axis=2)
        sc = (jnp.einsum('bhqd,bhkd->bhqk', qn, k_nope, preferred_element_type=F32)
              + jnp.einsum('bhqr,bkr->bhqk', qr, k_pe, preferred_element_type=F32)) * scale
        qpos = st + jnp.arange(ATTN_QBLOCK)
        sc = jnp.where(kpos[None, :] <= qpos[:, None], sc, -jnp.inf)
        p = jax.nn.softmax(sc, axis=-1).astype(v.dtype)
        return jnp.einsum('bhqk,bhkd->bhqd', p, v)

    out = lax.map(blk, jnp.arange(s // ATTN_QBLOCK))
    return out.transpose(1, 2, 0, 3, 4).reshape(b, h, s, B_VDIM)

def parallel_mixer(h, pos, w_in, q_lat_norm, w_uq, kv_lat_norm, w_ukv, w_branch_a, w_branch_b, w_out):
    splits = list(np.cumsum([A_WIDTH, A_WIDTH, A_WIDTH, B_Q_LORA, B_KV_LORA, B_ROPE, D_MODEL]))
    qa, ka, va, q_lat, kv_lat, k_pe, g_a, g_b = jnp.split(h @ w_in, splits, axis=-1)
    o_a = moba_attention(rope(_heads(qa, A_HEADS), pos), rope(_heads(ka, A_HEADS), pos), _heads(va, A_HEADS))
    q = _heads(rmsnorm(q_lat, q_lat_norm) @ w_uq, B_HEADS)
    q_nope, q_pe = q[..., :B_NOPE], rope(q[..., B_NOPE:], pos)
    kv = _heads(rmsnorm(kv_lat, kv_lat_norm) @ w_ukv, B_HEADS)
    k_nope, v_b = kv[..., :B_NOPE], kv[..., B_NOPE:]
    k_pe = rope(k_pe[:, None], pos)[:, 0]
    o_b = mla_attention(q_nope, q_pe, k_nope, k_pe, v_b)
    merged = (jax.nn.sigmoid(g_a) * (_merge(o_a) @ w_branch_a)
              + jax.nn.sigmoid(g_b) * (_merge(o_b) @ w_branch_b))
    return merged @ w_out

def memory_cross_attention(h, m, w_xq, w_xkv, w_xo):
    q = _heads(h @ w_xq, X_HEADS)
    k, v = jnp.split(m @ w_xkv, 2, axis=-1)
    k, v = _heads(k, X_HEADS), _heads(v, X_HEADS)
    sc = jnp.einsum('bhqd,bhkd->bhqk', q, k, preferred_element_type=F32) * (X_HEAD_DIM ** -0.5)
    p = jax.nn.softmax(sc, axis=-1).astype(v.dtype)
    return _merge(jnp.einsum('bhqk,bhkd->bhqd', p, v)) @ w_xo

def swiglu(h, w_gate_up, w_down):
    gt, up = jnp.split(h @ w_gate_up, 2, axis=-1)
    return (jax.nn.silu(gt) * up) @ w_down

def setup_inputs(seed: int = 0) -> dict:
    key = jax.random.key(seed)
    ks = jax.random.split(key, 24)
    out_scale = (2 * DEPTH) ** -0.5

    def dense(k, shape, fan_in, scale=1.0):
        return jax.random.normal(k, shape, F32) * (scale * fan_in ** -0.5)

    def gain(k, shape):
        return 1.0 + 0.05 * jax.random.normal(k, shape, F32)

    L = DEPTH
    offsets = jax.random.randint(ks[2], (BATCH,), 0, 1024, dtype=jnp.int32)
    positions = offsets[:, None] + jnp.arange(SEQ, dtype=jnp.int32)[None, :]
    return {
        "x": jax.random.normal(ks[0], (BATCH, SEQ, D_MODEL), F32),
        "mem": jax.random.normal(ks[1], (BATCH, MEM_LEN, D_MODEL), F32),
        "positions": positions,
        "norm_mix": gain(ks[3], (L, D_MODEL)),
        "w_in": dense(ks[4], (L, D_MODEL, IN_WIDTH), D_MODEL),
        "q_lat_norm": gain(ks[5], (L, B_Q_LORA)),
        "w_uq": dense(ks[6], (L, B_Q_LORA, B_HEADS * (B_NOPE + B_ROPE)), B_Q_LORA),
        "kv_lat_norm": gain(ks[7], (L, B_KV_LORA)),
        "w_ukv": dense(ks[8], (L, B_KV_LORA, B_HEADS * (B_NOPE + B_VDIM)), B_KV_LORA),
        "w_branch_a": dense(ks[9], (L, A_WIDTH, D_MODEL), A_WIDTH),
        "w_branch_b": dense(ks[10], (L, B_WIDTH, D_MODEL), B_WIDTH),
        "w_out": dense(ks[11], (L, D_MODEL, D_MODEL), D_MODEL, out_scale),
        "norm_xattn": gain(ks[12], (L, D_MODEL)),
        "norm_mem": gain(ks[13], (L, D_MODEL)),
        "w_xq": dense(ks[14], (L, D_MODEL, X_WIDTH), D_MODEL),
        "w_xkv": dense(ks[15], (L, D_MODEL, 2 * X_WIDTH), D_MODEL),
        "w_xo": dense(ks[16], (L, X_WIDTH, D_MODEL), X_WIDTH, out_scale),
        "norm_ffn": gain(ks[17], (L, D_MODEL)),
        "w_gate_up": dense(ks[18], (L, D_MODEL, 2 * D_FF), D_MODEL),
        "w_down": dense(ks[19], (L, D_FF, D_MODEL), D_FF, out_scale),
        "norm_final": gain(ks[20], (D_MODEL,)),
    }

def reference(x, mem, positions, norm_mix, w_in, q_lat_norm, w_uq, kv_lat_norm, w_ukv,
              w_branch_a, w_branch_b, w_out, norm_xattn, norm_mem, w_xq, w_xkv, w_xo,
              norm_ffn, w_gate_up, w_down, norm_final):
    for l in range(DEPTH):
        x = x + parallel_mixer(rmsnorm(x, norm_mix[l]), positions, w_in[l], q_lat_norm[l], w_uq[l],
                               kv_lat_norm[l], w_ukv[l], w_branch_a[l], w_branch_b[l], w_out[l])
        x = x + memory_cross_attention(rmsnorm(x, norm_xattn[l]), rmsnorm(mem, norm_mem[l]),
                                       w_xq[l], w_xkv[l], w_xo[l])
        x = x + swiglu(rmsnorm(x, norm_ffn[l]), w_gate_up[l], w_down[l])
    return rmsnorm(x, norm_final)


_drawn_inputs = setup_inputs


def setup_inputs(seed=0):
    import zlib

    import numpy as np

    out = dict(_drawn_inputs(seed))
    spreads = {}
    factors = {'norm_mix': 6.069,
     'q_lat_norm': 8.0,
     'kv_lat_norm': 8.0,
     'norm_xattn': 8.0,
     'norm_mem': 8.0}
    for name, (base, spread) in spreads.items():
        noise = np.random.default_rng([zlib.crc32(name.encode()), seed]).standard_normal(out[name].shape)
        drawn = base * np.exp(spread * noise) if base else spread * noise
        out[name] = __import__('jax').numpy.asarray(drawn.astype(out[name].dtype))
    for name, factor in factors.items():
        out[name] = (out[name] * factor).astype(out[name].dtype)
    return out
```

```python
from contextlib import ExitStack
import math

import numpy as np
import concourse.bass as bass
from concourse import mybir

F32 = mybir.dt.float32
F32R = mybir.dt.float32r
BF16 = mybir.dt.bfloat16
I32 = mybir.dt.int32
ALU = mybir.AluOpType
ACT = mybir.ActivationFunctionType
AX = mybir.AxisListType

P = 128
D = 1024
T = 256
TT = T // P
DEPTH = 2
DC = D // P
EPS = 1e-6
THETA = 10000.0
HA, DA = 8, 64
HB, NOPE, ROPE, VB = 8, 64, 32, 64
DB = NOPE + ROPE
QL, KL = 384, 256
LAT = QL + KL + ROPE
ZC = (QL + KL) // P
HX, DX = 4, 128
FF = 2816
FS = 256
NSLICE = FF // FS
HEADS = HA + HB
ALL_HEADS = HEADS + HX
SCALE_A = DA ** -0.5
SCALE_B = DB ** -0.5
SCALE_X = DX ** -0.5
MASKED = -1e30
Z_BANK = (6, 7, 0, 1, 2)
SPLIT = 2048

T_Q, T_K, T_LAT, T_V, T_UQ, T_UKV, T_GATE = 0, 2, 4, 7, 9, 11, 12
T_XK, T_BRANCH, T_OUT, T_XQ, T_XV, T_XO, T_FFN = 20, 22, 26, 30, 32, 34, 36
T_LOOP = T_FFN + 5
LOOPS = NSLICE - 2
T_LAST = T_LOOP + 3 * LOOPS
TILES = T_LAST + 1
SLOTS = 3
assert TILES % SLOTS == 0 and T_LOOP % SLOTS == 2

G_MIX, G_X, G_MEM, G_FFN, G_LAT = 0, DC, 2 * DC, 3 * DC, 4 * DC
GAINS = G_LAT + ZC

TURNS = HA // 2 + HB
TURN = []
_rest = 2 * math.pi
for _ in range(3):
    _part = math.ldexp(math.floor(math.ldexp(_rest, 8 - math.frexp(_rest)[1])), math.frexp(_rest)[1] - 8)
    TURN.append(_part)
    _rest -= _part
TURN.append(_rest)
ROUND = 1.5 * 2.0 ** 23
PI_LOW = float(np.nextafter(np.float32(math.pi), np.float32(0)))


def tile_cut(n):
    if n in (T_LAT, T_LAT + 1):
        return 3, LAT
    if n == T_LAT + 2:
        return 2, LAT
    if T_UQ <= n < T_UKV:
        return 3, 384
    if n == T_UKV:
        return 2, 1024
    if n < T_UQ or T_BRANCH <= n < T_OUT or T_XV <= n < T_FFN:
        return 4, 512
    if n == T_FFN + 3 or n == T_LAST:
        return 2, D
    return 8, 256


def turn_of(s):
    return s // 2 if s < HA else s - HA // 2


def last_head(u):
    return 2 * u + 1 if u < HA // 2 else u + HA // 2


class Steps:

    def __init__(self, eng, sem):
        self.eng, self.sem, self.base, self.n = eng, sem, 0, 0

    def start(self, base):
        self.base, self.n = base, 0

    def done(self, ins):
        self.n += 1
        ins.then_inc(self.sem, 1)
        self.eng.wait_ge(self.sem, self.base + self.n)


def trunk(nc, xT, memT, positions, freqs, gains, w_in, w_uq, w_ukv, w_branch_a, w_branch_b, w_out,
          w_xq, w_xkv, w_xo, w_gate_up, w_down, outT):
    with ExitStack() as ctx:
        def sb(name, shape, dt=F32):
            return ctx.enter_context(nc.sbuf_tensor(name, shape, dt))

        def sem(name):
            return ctx.enter_context(nc.semaphore(name))

        raw = [sb(f"raw{i}", [P, SPLIT]) for i in range(SLOTS)]
        w_hi = [sb(f"w_hi{i}", [P, SPLIT], F32R) for i in range(SLOTS)]
        w_lo = [sb(f"w_lo{i}", [P, SPLIT], F32R) for i in range(SLOTS)]
        x = sb("x", [P, DC, T])
        h_hi = sb("h_hi", [P, DC, T], F32R)
        h_lo = sb("h_lo", [P, DC, T], F32R)
        mem = sb("mem", [P, DC, T])
        m_hi = sb("m_hi", [P, DC, T], F32R)
        m_lo = sb("m_lo", [P, DC, T], F32R)
        a_hi = m_hi[:, 0:2, :]
        a_lo = m_lo[:, 0:2, :]
        q_a = sb("q_a", [P, TT, HA * DA])
        k_a = sb("k_a", [P, TT, HA * DA])
        v_a = sb("v_a", [P, TT, HA * DA])
        q_b = sb("q_b", [P, TT, HB, DB])
        k_b = sb("k_b", [P, TT, HB, DB])
        v_b = sb("v_b", [P, TT, HB, VB])
        xq = q_a[:, :, :].rearrange("p t n -> p (t n)").rearrange("p (h t) -> p h t", t=T)
        xk = k_a[:, :, :].rearrange("p t n -> p (t n)").rearrange("p (h t) -> p h t", t=T)
        xv = v_a
        oz = sb("oz", [P, 2, 8, T], F32R)
        z_hi, z_lo = oz[:, 0, 0:ZC, :], oz[:, 1, 0:ZC, :]
        o_hi, o_lo = oz[:, 0, :, :], oz[:, 1, :, :]
        region = sb("region", [P, 16, T])
        flat = region[:, :, :].rearrange("p a b -> p (a b)")
        z = flat[:, 0:TT * LAT].rearrange("p (t n) -> p t n", t=TT)
        z_sq = flat[:, TT * LAT:TT * LAT + TT * (QL + KL)].rearrange("p (t n) -> p t n", t=TT)
        gate = region
        xp = [region[:, 2 * j:2 * j + 2, :] for j in range(HX)]
        xpt = [region[:, 8 + 2 * j:10 + 2 * j, :] for j in range(2)]
        ff_g, ff_t, ff_m = (region[:, 2 * j:2 * j + 2, :] for j in range(3))
        y = region[:, 0:8, :]
        temp = sb("temp", [P, 4, 512])
        square_sum = sb("square_sum", [P, T])
        qk_t = [sb(f"qk_t{i}", [P, 4 * P]) for i in range(2)]
        prob = [sb(f"prob{i}", [P, 3 * P]) for i in range(2)]
        prob_t = [sb(f"prob_t{i}", [P, 3 * P]) for i in range(2)]
        row_max = [sb(f"row_max{i}", [P, TT]) for i in range(4)]
        bias = [sb(f"bias{i}", [P, TT]) for i in range(4)]
        row_sum = [sb(f"row_sum{i}", [P, TT]) for i in range(4)]
        row_inv = [sb(f"row_inv{i}", [P, TT]) for i in range(4)]
        rstd_both = sb("rstd_both", [P, T + TT])
        rstd_row = rstd_both[:, 0:T]
        rstd_col = rstd_both[:, T:T + TT]
        mem_rstd = sb("mem_rstd", [P, T + TT])
        mem_row, mem_col = mem_rstd[:, 0:T], mem_rstd[:, T:T + TT]
        x_scale = sb("x_scale", [P, TT])
        lat_ms = sb("lat_ms", [P, TT, 2])
        lat_rstd = sb("lat_rstd", [P, TT, 2])
        gain_all = sb("gain_all", [P, DEPTH * GAINS + DC])
        gain = sb("gain", [P, GAINS])
        freq = sb("freq", [P, 48])
        pos_i = sb("pos_i", [P, TT], I32)
        pos_f = sb("pos_f", [P, TT])
        angle, turns, trig = (q_b[:, :, :, :].rearrange("p t h n -> p (t h n)")[:, 192 * i:192 * i + 192]
                              .rearrange("p (f t n) -> p f t n", f=2, t=TT) for i in range(3))
        cos_a, sin_a = sb("cos_a", [P, TT, 64]), sb("sin_a", [P, TT, 64])
        cos_b, sin_b = sb("cos_b", [P, TT, 32]), sb("sin_b", [P, TT, 32])
        cos_ar, sin_ar = sb("cos_ar", [P, TT, 64]), sb("sin_ar", [P, TT, 64])
        cos_br, sin_br = sb("cos_br", [P, TT, 32]), sb("sin_br", [P, TT, 32])
        ident = sb("ident", [P, P])
        ident_h = sb("ident_h", [P, P], BF16)
        mask = sb("mask", [P, P], BF16)
        mean_of = sb("mean_of", [P, P])

        ps = ctx.enter_context(nc.psum_tensor("ps", [P, 8, 512], F32))

        raw_landed = [sem(f"raw_landed{i}") for i in range(SLOTS)]
        w_hi_done = sem("w_hi_done")
        w_lo_done = sem("w_lo_done")
        tile_used = sem("tile_used")
        x_loaded = sem("x_loaded")
        mem_loaded = sem("mem_loaded")
        const_loaded = sem("const_loaded")
        consts_made = sem("consts_made")
        x_ready = sem("x_ready")
        h_hi_done = sem("h_hi_done")
        h_lo_done = sem("h_lo_done")
        sums_ready = sem("sums_ready")
        stat_done = sem("stat_done")
        rstd_ready = sem("rstd_ready")
        gains_ready = sem("gains_ready")
        rope_mul = sem("rope_mul")
        rope_sum = sem("rope_sum")
        lat_copied = sem("lat_copied")
        lat_squared = sem("lat_squared")
        lat_rstd_ready = sem("lat_rstd_ready")
        kpe_mul = sem("kpe_mul")
        kpe_sum = sem("kpe_sum")
        z_turned = sem("z_turned")
        z_hi_done = sem("z_hi_done")
        z_lo_done = sem("z_lo_done")
        v_copied = sem("v_copied")
        qb_copied = sem("qb_copied")
        qb_mul = sem("qb_mul")
        qb_sum = sem("qb_sum")
        kb_copied = sem("kb_copied")
        vb_copied = sem("vb_copied")
        head_turned = sem("head_turned")
        head_copied = sem("head_copied")
        scored = sem("scored")
        max_ready = sem("max_ready")
        exp_done = sem("exp_done")
        prob_ready = sem("prob_ready")
        prob_turned = sem("prob_turned")
        prob_copied = sem("prob_copied")
        attended = sem("attended")
        o_hi_done = sem("o_hi_done")
        o_lo_done = sem("o_lo_done")
        gate_scaled = sem("gate_scaled")
        gate_tanh = sem("gate_tanh")
        m_hi_done = sem("m_hi_done")
        m_lo_done = sem("m_lo_done")
        xk_copied = sem("xk_copied")
        merge_ready = sem("merge_ready")
        merge_hi = sem("merge_hi")
        merge_lo = sem("merge_lo")
        xq_copied = sem("xq_copied")
        xv_copied = sem("xv_copied")
        g_scaled = sem("g_scaled")
        g_tanh = sem("g_tanh")
        hidden_gated = sem("hidden_gated")
        hidden_ready = sem("hidden_ready")
        a_hi_done = sem("a_hi_done")
        a_lo_done = sem("a_lo_done")
        final_sums = sem("final_sums")
        final_stat = sem("final_stat")
        y_ready = sem("y_ready")
        stored = sem("stored")
        pool_step = sem("pool_step")
        dve_step = sem("dve_step")
        act_step = sem("act_step")

        DVE_STEPS = 2 + 2 * ALL_HEADS + 4 + 1 + NSLICE + 4 * 10
        POOL_STEPS = 3 * 7

        def wide(row, n):
            return row.unsqueeze(1).broadcast_to([P, n, T])

        block = ctx.enter_context(nc.Block())

        @block.sync
        def _(sp):
            def kpn(w):
                return w.rearrange("l (c p) n -> l p c n", p=P)

            in_v, uq_v, ukv_v = kpn(w_in), kpn(w_uq), kpn(w_ukv)
            ba_v, bb_v, out_v = kpn(w_branch_a), kpn(w_branch_b), kpn(w_out)
            xq_v, xkv_v, xo_v = kpn(w_xq), kpn(w_xkv), kpn(w_xo)
            gu_v, down_v = kpn(w_gate_up), kpn(w_down)
            half = HX * DX

            def source(n):
                lat0 = 3 * HA * DA
                gate0 = lat0 + LAT
                if n < T_K:
                    return in_v, 4 * (n - T_Q), 0
                if n < T_LAT:
                    return in_v, 4 * (n - T_K), HA * DA
                if n < T_V:
                    return in_v, 3 * (n - T_LAT), lat0
                if n < T_UQ:
                    return in_v, 4 * (n - T_V), 2 * HA * DA
                if n < T_UKV:
                    return uq_v, 0, 384 * (n - T_UQ)
                if n < T_GATE:
                    return ukv_v, 0, 0
                if n < T_XK:
                    return in_v, 0, gate0 + 256 * (n - T_GATE)
                if n < T_BRANCH:
                    return xkv_v, 0, 256 * (n - T_XK)
                if n < T_OUT:
                    return (ba_v, bb_v)[(n - T_BRANCH) % 2], 0, 512 * ((n - T_BRANCH) // 2)
                if n < T_XQ:
                    return out_v, 0, 256 * (n - T_OUT)
                if n < T_XV:
                    return xq_v, 0, 256 * (n - T_XQ)
                if n < T_XO:
                    return xkv_v, 4 * (n - T_XV), half
                if n < T_FFN:
                    return xo_v, 0, 512 * (n - T_XO)
                return {T_FFN: (gu_v, 0, 0), T_FFN + 1: (gu_v, 0, FF), T_FFN + 2: (gu_v, 0, FS),
                        T_FFN + 3: (down_v, 0, 0), T_FFN + 4: (gu_v, 0, FF + FS),
                        T_LAST: (down_v, 2 * (NSLICE - 1), 0)}[n]

            def load(l, n):
                w, c0, col = source(n)
                c, m = tile_cut(n)
                dst = raw[n % SLOTS][:, 0:c * m].rearrange("p (c n) -> p c n", c=c)
                sp.dma_start(dst, w[l, :, c0:c0 + c, col:col + m]).then_inc(raw_landed[n % SLOTS], 16)

            for n in range(SLOTS):
                load(0, n)
            with_slots = [raw[i][:, :] for i in range(SLOTS)]
            with sp.Fori(0, DEPTH) as l:
                for n in range(T_LOOP - SLOTS):
                    sp.wait_ge(w_lo_done, l * TILES + n + 1)
                    load(l, n + SLOTS)
                with sp.Fori(0, LOOPS) as k:
                    for j in range(3):
                        sp.wait_ge(w_lo_done, l * TILES + k * 3 + (T_LOOP - SLOTS + j + 1))
                        slot = (T_LOOP + j) % SLOTS
                        if j == 1:
                            src = down_v[l, :, bass.ds(k * 2 + 2, 2), :]
                            dst = with_slots[slot].rearrange("p (c n) -> p c n", c=2)
                        else:
                            src = gu_v[l, :, :, bass.ds(k * FS + (2 * FS + (FF if j else 0)), FS)]
                            dst = with_slots[slot].rearrange("p (c n) -> p c n", c=8)
                        sp.dma_start(dst, src).then_inc(raw_landed[slot], 16)
                sp.wait_ge(w_lo_done, l * TILES + T_LAST - SLOTS + 1)
                load(l, T_LAST)
                following = (l + 1) % DEPTH
                for n in range(SLOTS):
                    sp.wait_ge(w_lo_done, l * TILES + T_LAST - 1 + n)
                    load(following, n)
            for j in range(4):
                sp.wait_ge(y_ready, 2 * j + 2)
                sp.dma_start(outT.rearrange("(c p) t -> p c t", p=P)[:, 2 * j:2 * j + 2, :],
                             y[:, 2 * j:2 * j + 2, :]).then_inc(stored, 16)
            for i in range(SLOTS):
                sp.wait_ge(raw_landed[i], 16 * (DEPTH * (TILES // SLOTS) + 1))
            sp.wait_ge(stored, 64)

        @block.gpsimd
        def _(pool):
            step = Steps(pool, pool_step)
            nc.gpsimd.memset(mean_of[:, :], 1.0 / D)
            nc.gpsimd.memset(ident[:, :], 0.0)
            nc.gpsimd.memset(ident_h[:, :], 0.0)
            step.done(nc.gpsimd.memset(mask[:, :], 0.0))
            for m in (ident, ident_h):
                nc.gpsimd.affine_select(out=m[:, :], in_=m[:, :], compare_op=ALU.not_equal, fill=1.0, base=0,
                                        pattern=[[-1, P]], channel_multiplier=1)
            nc.gpsimd.affine_select(out=mask[:, :], in_=mask[:, :], compare_op=ALU.is_ge, fill=MASKED, base=0,
                                    pattern=[[-1, P]], channel_multiplier=1).then_inc(consts_made, 1)

            def add_squares(src, ready, done):
                for p in range(4):
                    ready(p)
                    pair = src[:, 2 * p:2 * p + 2, :].rearrange("p c t -> p (c t)")
                    step.done(nc.gpsimd.tensor_tensor(temp[:, p, :], pair, pair, ALU.mult))
                    if p:
                        last = nc.gpsimd.tensor_tensor(temp[:, 0, :], temp[:, 0, :], temp[:, p, :], ALU.add)
                        step.done(last)
                nc.gpsimd.tensor_tensor(square_sum[:, :], temp[:, 0, 0:T], temp[:, 0, T:2 * T],
                                        ALU.add).then_inc(done, 1)

            add_squares(mem, lambda p: pool.wait_ge(mem_loaded, 16), sums_ready)
            pool.wait_ge(stat_done, 1)
            start = step.n
            with pool.Fori(0, DEPTH) as l:
                step.start(l * POOL_STEPS + start)
                add_squares(x, lambda p: pool.wait_ge(x_ready, l * 12 + p + 1), sums_ready)
                for i in range(4):
                    pool.wait_ge(rope_mul, l * 4 + i + 1)
                    out = (q_a, k_a)[i // 2][:, i % 2, :]
                    a = temp[:, 2 * (i % 2), :]
                    b = temp[:, 2 * (i % 2) + 1, :]
                    nc.gpsimd.tensor_tensor(out, a, b, ALU.add).then_inc(rope_sum, 1)
                pool.wait_ge(kpe_mul, l + 1)
                ka = temp[:, 0, 0:64].rearrange("p (t n) -> p t n", t=TT)
                kb = temp[:, 0, 64:128].rearrange("p (t n) -> p t n", t=TT)
                for t in range(TT):
                    last = nc.gpsimd.tensor_tensor(k_b[:, t, :, NOPE:DB],
                                                   ka[:, t, :].unsqueeze(1).broadcast_to([P, HB, ROPE]),
                                                   kb[:, t, :].unsqueeze(1).broadcast_to([P, HB, ROPE]), ALU.add)
                last.then_inc(kpe_sum, 1)
                for i in range(4):
                    pool.wait_ge(qb_mul, l * 4 + i + 1)
                    half, t = divmod(i, 2)
                    a = temp[:, 1 + i // 2, 256 * (i % 2):256 * (i % 2) + 128].rearrange("p (h n) -> p h n", h=4)
                    b = temp[:, 1 + i // 2, 256 * (i % 2) + 128:256 * (i % 2) + 256]\
                        .rearrange("p (h n) -> p h n", h=4)
                    nc.gpsimd.tensor_tensor(q_b[:, t, 4 * half:4 * half + 4, NOPE:DB], a, b,
                                            ALU.add).then_inc(qb_sum, 1)
                add_squares(x, lambda p: pool.wait_ge(x_ready, l * 12 + 4 + p + 1), sums_ready)
                add_squares(x, lambda p: pool.wait_ge(x_ready, l * 12 + 8 + p + 1), sums_ready)
            assert step.n == POOL_STEPS, step.n
            step.start(DEPTH * POOL_STEPS + start)
            add_squares(x, lambda p: pool.wait_ge(x_ready, DEPTH * 12 + p + 1), final_sums)

        @block.scalar
        def _(act):
            act.dma_start(x[:, :, :], xT.rearrange("(c p) t -> p c t", p=P)).then_inc(x_loaded, 16)
            act.dma_start(gain_all[:, :], gains).then_inc(const_loaded, 16)
            act.dma_start(freq[:, :], freqs).then_inc(const_loaded, 16)
            act.dma_start(pos_i[:, :], positions).then_inc(const_loaded, 16)
            act.dma_start(mem[:, :, :], memT.rearrange("(c p) t -> p c t", p=P)).then_inc(mem_loaded, 16)

            def split(l, n):
                act.wait_ge(raw_landed[n % SLOTS], (l * (TILES // SLOTS) + n // SLOTS + 1) * 16)
                if n >= SLOTS:
                    act.wait_ge(tile_used, l * TILES + (n - SLOTS + 2))
                elif n == 2:
                    act.wait_ge(tile_used, l * TILES + 1)
                c, m = tile_cut(n % TILES)
                nc.scalar.activation(w_hi[n % SLOTS][:, 0:c * m], raw[n % SLOTS][:, 0:c * m],
                                     ACT.Copy).then_inc(w_hi_done, 1)

            split(0, 0)
            split(0, 1)
            act.wait_ge(act_step, 1)
            nc.scalar.activation(trig[:, :, :, :], angle[:, :, :, :], ACT.Sin).then_inc(act_step, 1)

            def used(l, n):
                act.wait_ge(tile_used, l * TILES + n + 2)

            def h_split(l, norm, chunks, g0):
                for c in chunks:
                    if c % 2 == 0:
                        act.wait_ge(x_ready, l * 12 + 4 * norm + c // 2 + 1)
                    nc.scalar.activation(h_hi[:, c, :], x[:, c, :], ACT.Copy,
                                         scale=gain[:, g0 + c:g0 + c + 1]).then_inc(h_hi_done, 1)

            def head_copy(l, u):
                d = P if u < HA // 2 else DB
                act.wait_ge(head_turned, l * TURNS + u + 1)
                if u >= 2:
                    act.wait_ge(scored, l * ALL_HEADS + last_head(u - 2) + 1)
                nc.scalar.activation(qk_t[u % 2][0:d, :], ps[0:d, 5, :], ACT.Copy).then_inc(head_copied, 1)

            def head_exp(l, s):
                scale = SCALE_A if s < HA else SCALE_B
                act.wait_ge(max_ready, l * ALL_HEADS + s + 1)
                if s >= 2:
                    act.wait_ge(prob_turned, l * ALL_HEADS + s - 1)
                for t in range(TT):
                    cols = slice(0, P) if t == 0 else slice(P, 3 * P)
                    last = nc.scalar.activation(prob[s % 2][:, cols], ps[:, 6 + s % 2, cols], ACT.Exp,
                                                bias=bias[s % 2][:, t:t + 1], scale=scale,
                                                accum_out=row_sum[s % 2][:, t:t + 1])
                last.then_inc(exp_done, 1)

            def o_pair(l, r):
                act.wait_ge(attended, l * ALL_HEADS + 2 * r + 2)
                nc.scalar.activation(o_hi[:, r, :], ps[:, r % 2, 0:T], ACT.Copy).then_inc(o_hi_done, 1)

            def merge_split(l, p):
                act.wait_ge(merge_ready, l * 4 + p + 1)
                nc.scalar.activation(h_hi[:, 2 * p:2 * p + 2, :], gate[:, 2 * p:2 * p + 2, :],
                                     ACT.Copy).then_inc(merge_hi, 1)

            def hidden_tanh(i):
                act.wait_ge(g_scaled, i + 1)
                nc.scalar.activation(ff_t, ff_g, ACT.Tanh, scale=0.5).then_inc(g_tanh, 1)

            def hidden_split(i):
                act.wait_ge(hidden_ready, i + 1)
                nc.scalar.activation(a_hi, ff_m, ACT.Copy).then_inc(a_hi_done, 1)

            with act.Fori(0, DEPTH) as l:
                act.wait_ge(gains_ready, l + 1)
                h_split(l, 0, range(DC), G_MIX)
                for n in range(T_LAT + 3):
                    split(l, n + 2)
                used(l, T_LAT + 2)
                act.wait_ge(rstd_ready, l * 3 + 2)
                for t in range(TT):
                    for i in range(2):
                        nc.scalar.activation(z[:, t, 336 * i:336 * i + 336], ps[:, 2 * t + i, 0:336], ACT.Copy,
                                             scale=rstd_col[:, t:t + 1]).then_inc(lat_copied, 1)
                split(l, T_V + 2)
                act.wait_ge(lat_copied, l * 4 + 4)
                for t in range(TT):
                    for i, (a, b) in enumerate(((0, QL), (QL, QL + KL))):
                        nc.scalar.activation(z_sq[:, t, a:b], z[:, t, a:b], ACT.Square, scale=(b - a) ** -0.5,
                                             accum_out=lat_ms[:, t, i:i + 1]).then_inc(lat_squared, 1)
                for c in range(ZC):
                    act.wait_ge(z_turned, l * ZC + c + 1)
                    b = Z_BANK[c]
                    nc.scalar.activation(z_hi[:, c, :], ps[:, b, 0:T], ACT.Copy,
                                         scale=gain[:, G_LAT + c:G_LAT + c + 1]).then_inc(z_hi_done, 1)
                split(l, T_V + 3)
                used(l, T_V + 1)
                for t in range(TT):
                    nc.scalar.activation(v_a[:, t, :], ps[:, 4 + t, :], ACT.Copy,
                                         scale=rstd_col[:, t:t + 1]).then_inc(v_copied, 1)
                split(l, T_UQ + 2)
                act.wait_ge(lat_rstd_ready, l + 1)
                for i in range(2):
                    used(l, T_UQ + i)
                    for t in range(TT):
                        src = ps[:, 2 + 2 * i + t, 0:384].rearrange("p (h n) -> p h n", h=4)
                        nc.scalar.activation(q_b[:, t, 4 * i:4 * i + 4, 0:NOPE], src[:, :, 0:NOPE], ACT.Copy,
                                             scale=lat_rstd[:, t, 0:1]).then_inc(qb_copied, 1)
                    split(l, T_UQ + 3 + i)
                used(l, T_UKV)
                for t in range(TT):
                    for i in range(2):
                        src = ps[:, 6 * t + i, :].rearrange("p (h n) -> p h n", h=4)
                        nc.scalar.activation(k_b[:, t, 4 * i:4 * i + 4, 0:NOPE], src[:, :, 0:NOPE], ACT.Copy,
                                             scale=lat_rstd[:, t, 1:2]).then_inc(kb_copied, 1)
                head_copy(l, 0)
                for s in range(HEADS):
                    g = s // 2
                    head_exp(l, s)
                    if s % 2 == 0:
                        split(l, T_GATE + 2 + g)
                        if g >= 1:
                            o_pair(l, g - 1)
                            act.wait_ge(gate_scaled, l * 8 + g)
                            tile = gate[:, 2 * g - 2:2 * g, :]
                            nc.scalar.activation(tile, tile, ACT.Tanh, scale=0.5).then_inc(gate_tanh, 1)
                    else:
                        if g == 0:
                            used(l, T_GATE - 1)
                        nc.scalar.activation(m_hi[:, g, :], mem[:, g, :], ACT.Copy,
                                             scale=gain[:, G_MEM + g:G_MEM + g + 1]).then_inc(m_hi_done, 1)
                    if s + 1 < HEADS and turn_of(s + 1) != turn_of(s):
                        head_copy(l, turn_of(s + 1))
                act.wait_ge(gate_scaled, l * 8 + 8)
                nc.scalar.activation(gate[:, 14:16, :], gate[:, 14:16, :], ACT.Tanh, scale=0.5).then_inc(gate_tanh, 1)
                split(l, T_XK + 2)
                o_pair(l, HEADS // 2 - 1)
                split(l, T_XK + 3)
                split(l, T_BRANCH + 2)
                split(l, T_BRANCH + 3)
                merge_split(l, 0)
                merge_split(l, 1)
                split(l, T_BRANCH + 4)
                split(l, T_BRANCH + 5)
                merge_split(l, 2)
                merge_split(l, 3)
                for n in range(T_OUT, T_OUT + 4):
                    split(l, n + 2)
                used(l, T_OUT + 3)
                h_split(l, 1, range(DC), G_X)
                split(l, T_XQ + 2)
                for j in range(2):
                    used(l, T_XQ + j)
                    b = 4 + 2 * j
                    nc.scalar.activation(xq[:, 2 * j:2 * j + 2, :], ps[:, b:b + 2, 0:T], ACT.Copy).then_inc(xq_copied, 1)
                    if j == 0:
                        split(l, T_XQ + 3)
                for j in range(HX):
                    s = HEADS + j
                    act.wait_ge(max_ready, l * ALL_HEADS + s + 1)
                    for t in range(TT):
                        last = nc.scalar.activation(xp[j][:, t, :], ps[:, j, T * t:T * t + T], ACT.Exp,
                                                    bias=bias[j][:, t:t + 1], scale=x_scale[:, t:t + 1],
                                                    accum_out=row_sum[j][:, t:t + 1])
                    last.then_inc(exp_done, 1)
                    if j == 1:
                        split(l, T_XV + 2)
                split(l, T_XV + 3)
                used(l, T_XV + 1)
                for t in range(TT):
                    nc.scalar.activation(xv[:, t, :], ps[:, 6 + t, :], ACT.Copy,
                                         scale=mem_col[:, t:t + 1]).then_inc(xv_copied, 1)
                split(l, T_XO + 2)
                for r in range(2):
                    act.wait_ge(attended, l * ALL_HEADS + HEADS + 2 * r + 2)
                    nc.scalar.activation(o_hi[:, 2 * r:2 * r + 2, :],
                                         ps[:, 4 + r, :].rearrange("p (h t) -> p h t", h=2),
                                         ACT.Copy).then_inc(o_hi_done, 1)
                split(l, T_XO + 3)
                h_split(l, 2, range(4), G_FFN)
                h_split(l, 2, range(4, DC), G_FFN)
                split(l, T_FFN + 2)
                hidden_tanh(l * NSLICE)
                split(l, T_FFN + 3)
                hidden_split(l * NSLICE)
                split(l, T_FFN + 4)
                hidden_tanh(l * NSLICE + 1)
                split(l, T_FFN + 5)
                split(l, T_FFN + 6)
                with act.Fori(0, LOOPS) as k:
                    def loop_split(j):
                        slot = (T_LOOP + 2 + j) % SLOTS
                        n = T_LOOP + 2 + j
                        act.wait_ge(raw_landed[slot], (l * (TILES // SLOTS) + k + (n // SLOTS + 1)) * 16)
                        act.wait_ge(tile_used, l * TILES + k * 3 + (n - SLOTS + 2))
                        nc.scalar.activation(w_hi[slot][:, :], raw[slot][:, :], ACT.Copy).then_inc(w_hi_done, 1)
                    hidden_split(l * NSLICE + k + 1)
                    loop_split(0)
                    hidden_tanh(l * NSLICE + k + 2)
                    loop_split(1)
                    loop_split(2)
                hidden_split(l * NSLICE + (NSLICE - 1))
                split(l, TILES + 1)

        @block.vector
        def _(dve):
            step = Steps(dve, dve_step)
            V = nc.vector

            def split(l, n):
                dve.wait_ge(w_hi_done, l * TILES + n + 1)
                c, m = tile_cut(n % TILES)
                V.tensor_tensor(w_lo[n % SLOTS][:, 0:c * m], raw[n % SLOTS][:, 0:c * m],
                                w_hi[n % SLOTS][:, 0:c * m].bitcast(F32), ALU.subtract).then_inc(w_lo_done, 1)

            dve.wait_ge(const_loaded, 48)
            step.done(V.tensor_copy(pos_f[:, :], pos_i[:, :]))
            for t in range(TT):
                last = V.tensor_scalar(angle[:, 0, t, :], freq[:, :], pos_f[:, t:t + 1], None, ALU.mult)
            step.done(last)
            ang, cosine, trn = angle[:, 0, :, :], angle[:, 1, :, :], turns[:, 0, :, :]
            step.done(V.tensor_scalar(trn, ang, 1 / (2 * math.pi), ROUND, ALU.mult, ALU.add))
            step.done(V.tensor_scalar(trn, trn, ROUND, None, ALU.subtract))
            for part in TURN:
                step.done(V.scalar_tensor_tensor(out=ang, in0=trn, scalar=-part, in1=ang, op0=ALU.mult, op1=ALU.add))
            step.done(V.tensor_scalar(cosine, ang, math.pi / 2, None, ALU.add))
            step.done(V.tensor_scalar(trn, cosine, math.pi, -2 * math.pi, ALU.is_gt, ALU.mult))
            step.done(V.tensor_tensor(cosine, cosine, trn, ALU.add))
            V.tensor_scalar(angle[:, :, :, :], angle[:, :, :, :], PI_LOW, -PI_LOW, ALU.min,
                            ALU.max).then_inc(act_step, 1)
            dve.wait_ge(act_step, 2)
            for c_t, s_t, f0, m in ((cos_a, sin_a, 0, 32), (cos_b, sin_b, 32, 16)):
                V.tensor_copy(c_t[:, :, 0:m], trig[:, 1, :, f0:f0 + m])
                V.tensor_copy(c_t[:, :, m:2 * m], trig[:, 1, :, f0:f0 + m])
                V.tensor_scalar(s_t[:, :, 0:m], trig[:, 0, :, f0:f0 + m], -1.0, None, ALU.mult)
                last = V.tensor_copy(s_t[:, :, m:2 * m], trig[:, 0, :, f0:f0 + m])
            step.done(last)
            split(0, 0)
            split(0, 1)

            def rstd(y, src, work):
                n = src.shape[-1]
                v, t = work[:, 0:n], work[:, n:2 * n]
                step.done(V.tensor_scalar(v, src, EPS, None, ALU.add))
                step.done(V.tensor_scalar(y.bitcast(I32), v.bitcast(I32), -0.5, float(0x5F3759DF), ALU.mult, ALU.add))
                for i in range(3):
                    step.done(V.tensor_tensor(t, y, y, ALU.mult))
                    step.done(V.scalar_tensor_tensor(out=t, in0=t, scalar=-0.5, in1=v, op0=ALU.mult, op1=ALU.mult))
                    last = V.scalar_tensor_tensor(out=y, in0=t, scalar=1.5, in1=y, op0=ALU.add, op1=ALU.mult)
                    if i < 2:
                        step.done(last)
                return last

            work = temp[:, 2:4, :].rearrange("p a b -> p (a b)")
            dve.wait_ge(stat_done, 1)
            rstd(mem_rstd[:, :], ps[:, 0, 0:T + TT], q_b[:, :, :, :].rearrange("p t h n -> p (t h n)")[:, 768:1536])\
                .then_inc(rstd_ready, 1)
            dve.wait_ge(x_loaded, 16)
            dve.sem_inc(x_ready, 4)

            def used(l, n):
                dve.wait_ge(tile_used, l * TILES + n + 2)

            def h_split(l, norm, chunks, g0):
                for c in chunks:
                    dve.wait_ge(h_hi_done, l * 24 + 8 * norm + c + 1)
                    V.scalar_tensor_tensor(out=h_lo[:, c, :], in0=x[:, c, :], scalar=gain[:, g0 + c:g0 + c + 1],
                                           in1=h_hi[:, c, :].bitcast(F32), op0=ALU.mult,
                                           op1=ALU.subtract).then_inc(h_lo_done, 1)

            def swapped(ap, m):
                v = ap.rearrange("p (h j n) -> p h j n", j=2, n=m)
                return [v[:, :, 1, :], v[:, :, 0, :]]

            def rope_a(l, i):
                t = i % 2
                src = ps[:, 4 + i, :]
                if i >= 2:
                    dve.wait_ge(rope_sum, l * 4 + i - 1)
                V.tensor_tensor(temp[:, 2 * t, :].rearrange("p (h n) -> p h n", h=HA),
                                src.rearrange("p (h n) -> p h n", h=HA),
                                cos_ar[:, t, :].unsqueeze(1).broadcast_to([P, HA, DA]), ALU.mult)
                other = temp[:, 2 * t + 1, :].rearrange("p (h j n) -> p h j n", j=2, n=32)
                for j, part in enumerate(swapped(src, 32)):
                    last = V.tensor_tensor(other[:, :, j, :], part,
                                           sin_ar[:, t, 32 * j:32 * j + 32].unsqueeze(1).broadcast_to([P, HA, 32]),
                                           ALU.mult)
                last.then_inc(rope_mul, 1)

            def head_max(l, s):
                dve.wait_ge(scored, l * ALL_HEADS + s + 1)
                V.tensor_reduce(row_max[s % 2][:, 0:1], ps[:, 6 + s % 2, 0:P], AX.X, ALU.max)
                step.done(V.tensor_reduce(row_max[s % 2][:, 1:2], ps[:, 6 + s % 2, P:3 * P], AX.X, ALU.max))
                V.tensor_scalar(bias[s % 2][:, :], row_max[s % 2][:, :], -(SCALE_A if s < HA else SCALE_B), None,
                                ALU.mult).then_inc(max_ready, 1)

            def head_norm(l, s):
                dve.wait_ge(exp_done, l * ALL_HEADS + s + 1)
                step.done(V.reciprocal(row_inv[s % 2][:, :], row_sum[s % 2][:, :]))
                V.tensor_scalar(prob[s % 2][:, 0:P], prob[s % 2][:, 0:P], row_inv[s % 2][:, 0:1], None, ALU.mult)
                V.tensor_scalar(prob[s % 2][:, P:3 * P], prob[s % 2][:, P:3 * P], row_inv[s % 2][:, 1:2], None,
                                ALU.mult).then_inc(prob_ready, 1)

            def prob_copy(l, s):
                dve.wait_ge(prob_turned, l * ALL_HEADS + s + 1)
                if s >= 2:
                    dve.wait_ge(attended, l * ALL_HEADS + s - 1)
                V.tensor_copy(prob_t[s % 2][:, :], ps[:, 4, 0:3 * P]).then_inc(prob_copied, 1)

            def o_pair(l, r):
                dve.wait_ge(o_hi_done, l * 10 + r + 1)
                V.tensor_tensor(o_lo[:, r, :], ps[:, r % 2, 0:T], o_hi[:, r, :].bitcast(F32),
                                ALU.subtract).then_inc(o_lo_done, 1)

            def gate_scale(l, g):
                used(l, T_GATE + g)
                V.tensor_tensor(gate[:, 2 * g:2 * g + 2, :], ps[:, 2 + g % 2, :].rearrange("p (c t) -> p c t", c=2),
                                wide(rstd_row[:, :], 2), ALU.mult).then_inc(gate_scaled, 1)

            def banks(b):
                if isinstance(b, tuple):
                    return ps[:, b[0]:b[1] + 1, 0:T]
                return ps[:, b, :].rearrange("p (c t) -> p c t", c=2)

            def add_to_x(pair, b, factor):
                V.scalar_tensor_tensor(out=x[:, 2 * pair:2 * pair + 2, :], in0=banks(b), scalar=factor,
                                       in1=x[:, 2 * pair:2 * pair + 2, :], op0=ALU.mult,
                                       op1=ALU.add).then_inc(x_ready, 1)

            def gated(i, b, p):
                tile = gate[:, 8 * i + 2 * p:8 * i + 2 * p + 2, :]
                return V.scalar_tensor_tensor(out=tile, in0=tile, scalar=1.0, in1=banks(b), op0=ALU.add,
                                              op1=ALU.mult)

            def merge(l, p):
                a, b = gate[:, 2 * p:2 * p + 2, :], gate[:, 8 + 2 * p:10 + 2 * p, :]
                V.tensor_tensor(a, a, b, ALU.add).then_inc(merge_ready, 1)

            def merge_split(l, p):
                dve.wait_ge(merge_hi, l * 4 + p + 1)
                V.tensor_tensor(h_lo[:, 2 * p:2 * p + 2, :], gate[:, 2 * p:2 * p + 2, :],
                                h_hi[:, 2 * p:2 * p + 2, :].bitcast(F32), ALU.subtract).then_inc(merge_lo, 1)

            def hidden_scale(b):
                V.tensor_tensor(ff_g, banks(b), wide(rstd_row[:, :], 2), ALU.mult).then_inc(g_scaled, 1)

            def hidden_gate(i):
                dve.wait_ge(g_tanh, i + 1)
                step.done(V.scalar_tensor_tensor(out=ff_m, in0=ff_t, scalar=1.0, in1=ff_g, op0=ALU.add,
                                                 op1=ALU.mult))
                V.tensor_tensor(ff_m, ff_m, wide(rstd_row[:, :], 2), ALU.mult).then_inc(hidden_gated, 1)

            def hidden_times_up(i):
                dve.wait_ge(hidden_gated, i + 1)
                V.tensor_tensor(ff_m, ff_m, banks(5), ALU.mult).then_inc(hidden_ready, 1)
                dve.wait_ge(a_hi_done, i + 1)
                V.tensor_tensor(a_lo, ff_m, a_hi.bitcast(F32), ALU.subtract).then_inc(a_lo_done, 1)

            start = step.n
            with dve.Fori(0, DEPTH) as l:
                step.start(l * DVE_STEPS + start)
                V.tensor_copy(gain[:, :], gain_all[:, bass.ds(l * GAINS, GAINS)]).then_inc(gains_ready, 1)
                dve.wait_ge(gains_ready, l + 1)
                h_split(l, 0, range(DC), G_MIX)
                split(l, 2)
                split(l, 3)
                dve.wait_ge(stat_done, l * 3 + 2)
                rstd(rstd_both[:, :], ps[:, 0, 0:T + TT], work).then_inc(rstd_ready, 1)
                dve.wait_ge(rstd_ready, l * 3 + 2)
                for t in range(TT):
                    V.tensor_scalar(cos_ar[:, t, :], cos_a[:, t, :], rstd_col[:, t:t + 1], None, ALU.mult)
                    last = V.tensor_scalar(sin_ar[:, t, :], sin_a[:, t, :], rstd_col[:, t:t + 1], None, ALU.mult)
                step.done(last)
                used(l, T_Q + 1)
                rope_a(l, 0)
                rope_a(l, 1)
                split(l, 4)
                split(l, 5)
                used(l, T_K + 1)
                rope_a(l, 2)
                rope_a(l, 3)
                split(l, 6)
                split(l, 7)
                split(l, 8)
                split(l, 9)
                dve.wait_ge(lat_squared, l * 4 + 4)
                dve.wait_ge(rope_sum, l * 4 + 4)
                rstd(lat_rstd[:, :, :].rearrange("p t n -> p (t n)"), lat_ms[:, :, :].rearrange("p t n -> p (t n)"),
                     work).then_inc(lat_rstd_ready, 1)
                pe = z[:, :, QL + KL:LAT]
                V.tensor_tensor(temp[:, 0, 0:64].rearrange("p (t n) -> p t n", t=TT), pe, cos_b[:, :, :], ALU.mult)
                other = temp[:, 0, 64:128].rearrange("p (t n) -> p t n", t=TT)
                V.tensor_tensor(other[:, :, 0:16], pe[:, :, 16:32], sin_b[:, :, 0:16], ALU.mult)
                V.tensor_tensor(other[:, :, 16:32], pe[:, :, 0:16], sin_b[:, :, 16:32], ALU.mult).then_inc(kpe_mul, 1)
                dve.wait_ge(lat_rstd_ready, l + 1)
                for t in range(TT):
                    V.tensor_scalar(cos_br[:, t, :], cos_b[:, t, :], lat_rstd[:, t, 0:1], None, ALU.mult)
                    last = V.tensor_scalar(sin_br[:, t, :], sin_b[:, t, :], lat_rstd[:, t, 0:1], None, ALU.mult)
                step.done(last)
                for c in range(ZC):
                    dve.wait_ge(z_hi_done, l * ZC + c + 1)
                    b = Z_BANK[c]
                    V.scalar_tensor_tensor(out=z_lo[:, c, :], in0=ps[:, b, 0:T],
                                           scalar=gain[:, G_LAT + c:G_LAT + c + 1],
                                           in1=z_hi[:, c, :].bitcast(F32), op0=ALU.mult,
                                           op1=ALU.subtract).then_inc(z_lo_done, 1)
                split(l, T_V + 3)
                split(l, T_UQ + 2)
                for i in range(2):
                    for t in range(TT):
                        dve.wait_ge(qb_copied, l * 4 + 2 * i + t + 1)
                        src = ps[:, 2 + 2 * i + t, 0:384].rearrange("p (h n) -> p h n", h=4)
                        own = temp[:, 1 + i, 256 * t:256 * t + 128].rearrange("p (h n) -> p h n", h=4)
                        other = temp[:, 1 + i, 256 * t + 128:256 * t + 256].rearrange("p (h n) -> p h n", h=4)
                        V.tensor_tensor(own, src[:, :, NOPE:DB],
                                        cos_br[:, t, :].unsqueeze(1).broadcast_to([P, 4, ROPE]), ALU.mult)
                        for j in range(2):
                            last = V.tensor_tensor(
                                other[:, :, 16 * j:16 * j + 16], src[:, :, DB - 16 - 16 * j:DB - 16 * j],
                                sin_br[:, t, 16 * j:16 * j + 16].unsqueeze(1).broadcast_to([P, 4, 16]), ALU.mult)
                        last.then_inc(qb_mul, 1)
                    split(l, T_UQ + 3 + i)
                for t in range(TT):
                    for i in range(2):
                        dve.wait_ge(kb_copied, l * 4 + 2 * t + i + 1)
                        src = ps[:, 6 * t + i, :].rearrange("p (h n) -> p h n", h=4)
                        V.tensor_scalar(v_b[:, t, 4 * i:4 * i + 4, :], src[:, :, NOPE:NOPE + VB],
                                        lat_rstd[:, t, 1:2], None, ALU.mult).then_inc(vb_copied, 1)
                for s in range(HEADS):
                    g = s // 2
                    if s:
                        prob_copy(l, s - 1)
                    head_max(l, s)
                    if s % 2 == 0:
                        if g >= 1:
                            gate_scale(l, g - 1)
                        head_norm(l, s)
                        split(l, T_GATE + 2 + g)
                        if g >= 1:
                            o_pair(l, g - 1)
                    else:
                        head_norm(l, s)
                        dve.wait_ge(m_hi_done, l * 8 + g + 1)
                        V.scalar_tensor_tensor(out=m_lo[:, g, :], in0=mem[:, g, :],
                                               scalar=gain[:, G_MEM + g:G_MEM + g + 1],
                                               in1=m_hi[:, g, :].bitcast(F32), op0=ALU.mult,
                                               op1=ALU.subtract).then_inc(m_lo_done, 1)
                prob_copy(l, HEADS - 1)
                gate_scale(l, 7)
                split(l, T_XK + 2)
                o_pair(l, HEADS // 2 - 1)
                for j in range(2):
                    used(l, T_XK + j)
                    V.tensor_tensor(xk[:, 2 * j:2 * j + 2, :], banks(2 + j), wide(mem_row[:, :], 2),
                                    ALU.mult).then_inc(xk_copied, 1)
                    split(l, T_XK + 3 + j)
                used(l, T_BRANCH)
                dve.wait_ge(gate_tanh, l * 8 + 8)
                gated(0, 6, 0)
                gated(0, 7, 1)
                split(l, T_BRANCH + 3)
                used(l, T_BRANCH + 1)
                for p in range(2):
                    step.done(gated(1, 4 + p, p))
                    merge(l, p)
                for p in range(2):
                    merge_split(l, p)
                split(l, T_BRANCH + 4)
                used(l, T_BRANCH + 2)
                gated(0, 0, 2)
                gated(0, 1, 3)
                split(l, T_BRANCH + 5)
                used(l, T_BRANCH + 3)
                for p in range(2, 4):
                    step.done(gated(1, p, p))
                    merge(l, p)
                for p in range(2, 4):
                    merge_split(l, p)
                split(l, T_OUT + 2)
                for j, b in enumerate(((4, 5), (6, 7), (0, 1), (2, 3))):
                    used(l, T_OUT + j)
                    add_to_x(j, b, 0.5)
                    if j < 3:
                        split(l, T_OUT + 3 + j)
                h_split(l, 1, range(DC), G_X)
                split(l, T_XQ + 2)
                dve.wait_ge(stat_done, l * 3 + 3)
                step.done(rstd(rstd_col, ps[:, 0, T:T + TT], work))
                V.tensor_scalar(x_scale[:, :], rstd_col[:, :], SCALE_X, None, ALU.mult).then_inc(rstd_ready, 1)
                dve.wait_ge(rstd_ready, l * 3 + 3)
                split(l, T_XQ + 3)

                def x_norm(j):
                    dve.wait_ge(exp_done, l * ALL_HEADS + HEADS + j + 1)
                    step.done(V.reciprocal(row_inv[j][:, :], row_sum[j][:, :]))
                    for t in range(TT):
                        last = V.tensor_scalar(xp[j][:, t, :], xp[j][:, t, :], row_inv[j][:, t:t + 1], None, ALU.mult)
                    last.then_inc(prob_ready, 1)

                for j in range(HX):
                    dve.wait_ge(scored, l * ALL_HEADS + HEADS + j + 1)
                    step.done(V.tensor_reduce(row_max[j][:, :], ps[:, j, :].rearrange("p (t k) -> p t k", t=TT), AX.X,
                                              ALU.max))
                    V.scalar_tensor_tensor(out=bias[j][:, :], in0=row_max[j][:, :], scalar=-1.0, in1=x_scale[:, :],
                                           op0=ALU.mult, op1=ALU.mult).then_inc(max_ready, 1)
                x_norm(0)
                x_norm(1)
                split(l, T_XV + 2)
                x_norm(2)
                x_norm(3)
                split(l, T_XV + 3)
                for j in range(HX):
                    dve.wait_ge(prob_turned, l * ALL_HEADS + HEADS + j + 1)
                    if j >= 2:
                        dve.wait_ge(attended, l * ALL_HEADS + HEADS + j - 1)
                    V.tensor_copy(xpt[j % 2].rearrange("p a b -> p (a b)"), ps[:, j, :]).then_inc(prob_copied, 1)
                for r in range(2):
                    dve.wait_ge(o_hi_done, l * 10 + 8 + r + 1)
                    V.tensor_tensor(o_lo[:, 2 * r:2 * r + 2, :], banks(4 + r),
                                    o_hi[:, 2 * r:2 * r + 2, :].bitcast(F32), ALU.subtract).then_inc(o_lo_done, 1)
                split(l, T_XO + 2)
                used(l, T_XO)
                add_to_x(0, 6, 1.0)
                add_to_x(1, 7, 1.0)
                split(l, T_XO + 3)
                h_split(l, 2, range(4), G_FFN)
                used(l, T_XO + 1)
                add_to_x(2, 0, 1.0)
                add_to_x(3, 1, 1.0)
                h_split(l, 2, range(4, DC), G_FFN)
                split(l, T_FFN + 2)
                dve.wait_ge(stat_done, l * 3 + 4)
                rstd(rstd_row, ps[:, 4, 0:T], work).then_inc(rstd_ready, 1)
                dve.wait_ge(rstd_ready, l * 3 + 4)
                used(l, T_FFN)
                hidden_scale((6, 7))
                hidden_gate(l * NSLICE)
                split(l, T_FFN + 3)
                used(l, T_FFN + 1)
                dve.wait_ge(rstd_ready, l * 3 + 4)
                hidden_times_up(l * NSLICE)
                split(l, T_FFN + 4)
                used(l, T_FFN + 2)
                hidden_scale(4)
                split(l, T_FFN + 5)
                hidden_gate(l * NSLICE + 1)
                split(l, T_FFN + 6)
                done = step.n
                with dve.Fori(0, LOOPS) as k:
                    def loop_split(j):
                        slot = (T_LOOP + 2 + j) % SLOTS
                        dve.wait_ge(w_hi_done, l * TILES + k * 3 + (T_LOOP + 2 + j + 1))
                        V.tensor_tensor(w_lo[slot][:, :], raw[slot][:, :], w_hi[slot][:, :].bitcast(F32),
                                        ALU.subtract).then_inc(w_lo_done, 1)
                    step.start(l * DVE_STEPS + k + (start + done))
                    dve.wait_ge(tile_used, l * TILES + k * 3 + (T_LOOP - 1 + 2))
                    hidden_times_up(l * NSLICE + k + 1)
                    loop_split(0)
                    dve.wait_ge(tile_used, l * TILES + k * 3 + (T_LOOP + 2))
                    hidden_scale(4)
                    loop_split(1)
                    hidden_gate(l * NSLICE + k + 2)
                    loop_split(2)
                assert step.n == 1 and done + LOOPS == DVE_STEPS, (step.n, done + LOOPS, DVE_STEPS)
                used(l, T_LAST - 1)
                hidden_times_up(l * NSLICE + (NSLICE - 1))
                split(l, TILES + 1)
                used(l, T_LAST)
                for p in range(4):
                    add_to_x(p, p, 0.5)
            dve.wait_ge(final_stat, 1)
            step.start(DEPTH * DVE_STEPS + start)
            rstd(rstd_row, ps[:, 4, 0:T], work).then_inc(final_stat, 1)
            dve.wait_ge(final_stat, 2)
            for c in range(DC):
                V.scalar_tensor_tensor(out=y[:, c, :], in0=x[:, c, :],
                                       scalar=gain_all[:, DEPTH * GAINS + c:DEPTH * GAINS + c + 1],
                                       in1=rstd_row[:, :], op0=ALU.mult, op1=ALU.mult).then_inc(y_ready, 1)

        @block.tensor
        def _(pe):
            mm = nc.tensor.matmul

            def cut(n):
                c, m = tile_cut(n)
                hi = w_hi[n % SLOTS][:, 0:c * m].rearrange("p (c n) -> p c n", c=c)
                lo = w_lo[n % SLOTS][:, 0:c * m].rearrange("p (c n) -> p c n", c=c)
                return hi, lo

            def by_token(n, a_hi, a_lo, c0, outs, first, last):
                hi, lo = cut(n)
                chunks = tile_cut(n)[0]
                for c in range(chunks):
                    for t in range(TT):
                        ah = a_hi[:, c0 + c, t * P:t * P + P]
                        al = a_lo[:, c0 + c, t * P:t * P + P]
                        for b, col, m in outs[t]:
                            begin, end = first and c == 0, last and c == chunks - 1
                            out = ps[:, b, 0:m]
                            mm(out, ah, hi[:, c, col:col + m], start=begin, stop=False)
                            mm(out, ah, lo[:, c, col:col + m], start=False, stop=False)
                            ins = mm(out, al, hi[:, c, col:col + m], start=False, stop=end)
                return ins

            def three(out, hi, lo, c, col, ah, al, begin, end, open_bank=False):
                wh, wl = hi[:, c, col:col + P], lo[:, c, col:col + P]
                mm(out, wh, ah, start=begin, stop=False, skip_group_check=open_bank)
                mm(out, wh, al, start=False, stop=False, skip_group_check=open_bank)
                return mm(out, wl, ah, start=False, stop=end, skip_group_check=open_bank)

            def by_feature(n, a_hi, a_lo, outs, before=None):
                hi, lo = cut(n)
                chunks = tile_cut(n)[0]
                for j, out in enumerate(outs):
                    for c in range(chunks):
                        if before and j == 0:
                            before(c)
                        ins = three(out, hi, lo, c, P * j, a_hi[:, c, :], a_lo[:, c, :], c == 0, c == chunks - 1)
                return ins

            def as_chunks_come(n, a_hi, a_lo, outs, before):
                hi, lo = cut(n)
                for c in range(DC):
                    before(c)
                    for j, out in enumerate(outs):
                        ins = three(out, hi, lo, c, P * j, a_hi[:, c, :], a_lo[:, c, :], c == 0, c == DC - 1)
                return ins

            def halves(b):
                return [ps[:, b, 0:T], ps[:, b, T:2 * T]]

            def split_done(l, n):
                pe.wait_ge(w_lo_done, l * TILES + n + 1)

            def h_ready(l, norm, c):
                pe.wait_ge(h_lo_done, l * 24 + 8 * norm + c + 1)

            def statistics(sums, value, b, done, row=True, col=True):
                pe.wait_ge(sums, value)
                if row:
                    ins = mm(ps[:, b, 0:T], mean_of[:, :], square_sum[:, :], start=True, stop=True)
                if col:
                    for t in range(TT):
                        ins = mm(ps[:, b, T + t:T + t + 1], square_sum[:, t * P:t * P + P], mean_of[:, 0:1],
                                 start=True, stop=True)
                ins.then_inc(done, 1)

            def turn_head(l, u):
                if u == 0:
                    pe.wait_ge(rope_sum, l * 4 + 4)
                    pe.wait_ge(qb_copied, l * 4 + 4)
                    pe.wait_ge(qb_mul, l * 4 + 4)
                else:
                    pe.wait_ge(head_copied, l * TURNS + u)
                if u == HA // 2:
                    pe.wait_ge(qb_sum, l * 4 + 4)
                    pe.wait_ge(kpe_sum, l + 1)
                d = P if u < HA // 2 else DB
                for i in range(4):
                    t = i % 2
                    if u < HA // 2:
                        src = (q_a, k_a)[i // 2][:, t, P * u:P * u + P]
                    else:
                        src = (q_b, k_b)[i // 2][:, t, u - HA // 2, :]
                    ins = nc.tensor.transpose(ps[0:d, 5, P * i:P * i + P], src, ident[:, :])
                ins.then_inc(head_turned, 1)

            def score(l, s):
                u = turn_of(s)
                d = slice(DA * (s % 2), DA * (s % 2) + DA) if s < HA else slice(0, DB)
                pe.wait_ge(head_copied, l * TURNS + u + 1)
                if s >= 2:
                    pe.wait_ge(exp_done, l * ALL_HEADS + s - 1)
                src, b = qk_t[u % 2], 6 + s % 2
                mm(ps[:, b, 0:P], src[d, 0:P], src[d, 2 * P:3 * P], start=True, stop=False)
                mm(ps[:, b, 0:P], ident_h[:, :], mask[:, :], start=False, stop=True)
                mm(ps[:, b, P:3 * P], src[d, P:2 * P], src[d, 2 * P:4 * P], start=True, stop=False)
                mm(ps[:, b, 2 * P:3 * P], ident_h[:, :], mask[:, :], start=False, stop=True).then_inc(scored, 1)

            def turn_prob(l, s):
                pe.wait_ge(prob_ready, l * ALL_HEADS + s + 1)
                if s:
                    pe.wait_ge(prob_copied, l * ALL_HEADS + s)
                for i in range(3):
                    ins = nc.tensor.transpose(ps[:, 4, P * i:P * i + P], prob[s % 2][:, P * i:P * i + P], ident[:, :])
                ins.then_inc(prob_turned, 1)

            def attend(l, s):
                pe.wait_ge(prob_copied, l * ALL_HEADS + s + 1)
                r = s // 2
                if r >= 2 and s % 2 == 0:
                    pe.wait_ge(o_lo_done, l * 10 + r - 1)
                part = slice(64 * (s % 2), 64 * (s % 2) + 64)
                v = [v_a[:, t, DA * s:DA * s + DA] if s < HA else v_b[:, t, s - HA, :] for t in range(TT)]
                mm(ps[part, r % 2, 0:T], v[0], prob_t[s % 2][:, 0:T], start=True, stop=False)
                mm(ps[part, r % 2, P:T], v[1], prob_t[s % 2][:, T:T + P], start=False,
                   stop=True).then_inc(attended, 1)

            pe.wait_ge(consts_made, 1)
            statistics(sums_ready, 1, 0, stat_done)
            pe.sem_inc(tile_used, 1)
            with pe.Fori(0, DEPTH) as l:
                for i in range(2):
                    split_done(l, T_Q + i)
                    hi, lo = cut(T_Q + i)
                    for c in range(4):
                        h_ready(l, 0, 4 * i + c)
                        for t in range(TT):
                            ah = h_hi[:, 4 * i + c, t * P:t * P + P]
                            al = h_lo[:, 4 * i + c, t * P:t * P + P]
                            mm(ps[:, 4 + t, :], ah, hi[:, c, :], start=(i + c == 0), stop=False)
                            mm(ps[:, 4 + t, :], ah, lo[:, c, :], start=False, stop=False)
                            ins = mm(ps[:, 4 + t, :], al, hi[:, c, :], start=False, stop=(i == 1 and c == 3))
                    ins.then_inc(tile_used, 1)
                pe.wait_ge(rstd_ready, l * 3 + 1)
                statistics(sums_ready, l * 3 + 2, 0, stat_done)
                for i in range(2):
                    split_done(l, T_K + i)
                    by_token(T_K + i, h_hi, h_lo, 4 * i, [[(6, 0, 512)], [(7, 0, 512)]], i == 0,
                             i == 1).then_inc(tile_used, 1)
                pe.wait_ge(rstd_ready, l * 3 + 2)
                for i in range(3):
                    split_done(l, T_LAT + i)
                    by_token(T_LAT + i, h_hi, h_lo, 3 * i, [[(2 * t + j, 336 * j, 336) for j in range(2)]
                                                           for t in range(TT)], i == 0, i == 2).then_inc(tile_used, 1)
                pe.wait_ge(rope_mul, l * 4 + 2)
                for i in range(2):
                    split_done(l, T_V + i)
                    by_token(T_V + i, h_hi, h_lo, 4 * i, [[(4, 0, 512)], [(5, 0, 512)]], i == 0,
                             i == 1).then_inc(tile_used, 1)
                    if i == 0:
                        pe.wait_ge(lat_copied, l * 4 + 4)
                        pe.wait_ge(rope_mul, l * 4 + 4)
                        for c in range(ZC):
                            b = Z_BANK[c]
                            for t in range(TT):
                                ins = nc.tensor.transpose(ps[:, b, t * P:t * P + P],
                                                          z[:, t, c * P:c * P + P], ident[:, :])
                            ins.then_inc(z_turned, 1)
                pe.wait_ge(z_lo_done, l * ZC + ZC)
                for i in range(2):
                    split_done(l, T_UQ + i)
                    if i == 1:
                        pe.wait_ge(v_copied, l * 2 + 2)
                    by_token(T_UQ + i, z_hi, z_lo, 0, [[(2 + 2 * i + t, 0, 384)] for t in range(TT)], True,
                             True).then_inc(tile_used, 1)
                split_done(l, T_UKV)
                by_token(T_UKV, z_hi, z_lo, 3, [[(6 * t + j, 512 * j, 512) for j in range(2)] for t in range(TT)],
                         True, True).then_inc(tile_used, 1)
                turn_head(l, 0)
                pe.wait_ge(kb_copied, l * 4 + 4)
                pe.wait_ge(vb_copied, l * 4 + 4)
                for s in range(HEADS):
                    g, j = divmod(s, 2)
                    score(l, s)
                    if s:
                        attend(l, s - 1)
                    if j == 0:
                        split_done(l, T_GATE + g)
                        if g >= 2:
                            pe.wait_ge(gate_scaled, l * 8 + g - 1)
                    hi, lo = cut(T_GATE + g)
                    for c in range(DC):
                        ins = three(halves(2 + g % 2)[j], hi, lo, c, P * j, h_hi[:, c, :], h_lo[:, c, :], c == 0,
                                    c == DC - 1)
                    if j == 1:
                        ins.then_inc(tile_used, 1)
                    if s + 1 < HEADS and turn_of(s + 1) != turn_of(s):
                        turn_head(l, turn_of(s + 1))
                    turn_prob(l, s)
                pe.wait_ge(m_lo_done, l * 8 + 8)
                for j in range(2):
                    pe.wait_ge(gate_scaled, l * 8 + 7 + j)
                    split_done(l, T_XK + j)
                    by_feature(T_XK + j, m_hi, m_lo, halves(2 + j)).then_inc(tile_used, 1)
                    if j == 0:
                        attend(l, HEADS - 1)
                for i, bank in enumerate((6, 4, 0, 2)):
                    split_done(l, T_BRANCH + i)
                    pe.wait_ge(o_lo_done, l * 10 + (4 if i == 0 else 8))
                    if i == 3:
                        pe.wait_ge(xk_copied, l * 2 + 2)
                    c0 = 4 * (i % 2)
                    by_feature(T_BRANCH + i, o_hi[:, c0:c0 + 4, :], o_lo[:, c0:c0 + 4, :],
                               halves(bank) + halves(bank + 1)).then_inc(tile_used, 1)
                for j, bank in enumerate((4, 6, 0, 2)):
                    split_done(l, T_OUT + j)
                    as_chunks_come(T_OUT + j, h_hi, h_lo, [ps[:, bank, 0:T], ps[:, bank + 1, 0:T]],
                                   lambda c: pe.wait_ge(merge_lo, l * 4 + max(2, c // 2 + 1))
                                   if j == 0 and c % 2 == 0 else None).then_inc(tile_used, 1)
                for j, bank in enumerate((4, 6)):
                    split_done(l, T_XQ + j)
                    as_chunks_come(T_XQ + j, h_hi, h_lo, [ps[:, bank, 0:T], ps[:, bank + 1, 0:T]],
                                   lambda c: h_ready(l, 1, c) if j == 0 else None).then_inc(tile_used, 1)
                    if j == 0:
                        statistics(sums_ready, l * 3 + 3, 0, stat_done, row=False)
                pe.wait_ge(rstd_ready, l * 3 + 3)
                for j in range(HX):
                    pe.wait_ge(xq_copied, l * 2 + j // 2 + 1)
                    for t in range(TT):
                        ins = mm(ps[:, j, t * T:t * T + T], xq[:, j, t * P:t * P + P], xk[:, j, :], start=True,
                                 stop=True)
                    ins.then_inc(scored, 1)
                for i in range(2):
                    split_done(l, T_XV + i)
                    by_token(T_XV + i, m_hi, m_lo, 4 * i, [[(6, 0, 512)], [(7, 0, 512)]], i == 0,
                             i == 1).then_inc(tile_used, 1)

                def x_turn(j):
                    pe.wait_ge(prob_ready, l * ALL_HEADS + HEADS + j + 1)
                    for kt in range(TT):
                        for t in range(TT):
                            ins = nc.tensor.transpose(ps[:, j, kt * T + t * P:kt * T + t * P + P],
                                                      xp[j][:, t, kt * P:kt * P + P], ident[:, :])
                    ins.then_inc(prob_turned, 1)

                def x_attend(j):
                    pe.wait_ge(prob_copied, l * ALL_HEADS + HEADS + j + 1)
                    if j == 0:
                        pe.wait_ge(xv_copied, l * 2 + 2)
                    for kt in range(TT):
                        ins = mm(halves(4 + j // 2)[j % 2], xv[:, kt, j * DX:j * DX + DX], xpt[j % 2][:, kt, :],
                                 start=(kt == 0), stop=(kt == TT - 1))
                    ins.then_inc(attended, 1)

                x_turn(0)
                for j in range(HX):
                    if j + 1 < HX:
                        x_turn(j + 1)
                    x_attend(j)
                for i, bank in enumerate((6, 0)):
                    split_done(l, T_XO + i)
                    pe.wait_ge(o_lo_done, l * 10 + 10)
                    by_feature(T_XO + i, o_hi, o_lo, halves(bank) + halves(bank + 1)).then_inc(tile_used, 1)

                def down(slot, first=False, last=False):
                    hi = w_hi[slot][:, :].rearrange("p (c n) -> p c n", c=2)
                    lo = w_lo[slot][:, :].rearrange("p (c n) -> p c n", c=2)
                    for m in range(DC):
                        for c in range(2):
                            ins = three(halves(m // 2)[m % 2], hi, lo, c, P * m, a_hi_v[:, c, :], a_lo_v[:, c, :],
                                        first and c == 0 and m % 2 == 0, last and c == 1, open_bank=True)
                    return ins

                a_hi_v, a_lo_v = a_hi, a_lo
                split_done(l, T_FFN)
                h_ready(l, 2, 2)
                as_chunks_come(T_FFN, h_hi, h_lo, [ps[:, 6, 0:T], ps[:, 7, 0:T]],
                               lambda c: h_ready(l, 2, c)).then_inc(tile_used, 1)
                statistics(sums_ready, l * 3 + 4, 4, stat_done, col=False)
                split_done(l, T_FFN + 1)
                by_feature(T_FFN + 1, h_hi, h_lo, halves(5)).then_inc(tile_used, 1)
                pe.wait_ge(rstd_ready, l * 3 + 4)
                split_done(l, T_FFN + 2)
                by_feature(T_FFN + 2, h_hi, h_lo, halves(4)).then_inc(tile_used, 1)
                split_done(l, T_FFN + 3)
                pe.wait_ge(a_lo_done, l * NSLICE + 1)
                down((T_FFN + 3) % SLOTS, first=True).then_inc(tile_used, 1)
                split_done(l, T_FFN + 4)
                by_feature(T_FFN + 4, h_hi, h_lo, halves(5)).then_inc(tile_used, 1)
                with pe.Fori(0, LOOPS) as k:
                    pe.wait_ge(w_lo_done, l * TILES + k * 3 + (T_LOOP + 1))
                    pe.wait_ge(g_scaled, l * NSLICE + k + 2)
                    by_feature(T_LOOP, h_hi, h_lo, halves(4)).then_inc(tile_used, 1)
                    pe.wait_ge(w_lo_done, l * TILES + k * 3 + (T_LOOP + 2))
                    pe.wait_ge(a_lo_done, l * NSLICE + k + 2)
                    down((T_LOOP + 1) % SLOTS).then_inc(tile_used, 1)
                    pe.wait_ge(w_lo_done, l * TILES + k * 3 + (T_LOOP + 3))
                    by_feature(T_LOOP + 2, h_hi, h_lo, halves(5)).then_inc(tile_used, 1)
                split_done(l, T_LAST)
                pe.wait_ge(a_lo_done, l * NSLICE + NSLICE)
                down(T_LAST % SLOTS, last=True).then_inc(tile_used, 1)
            statistics(final_sums, 1, 4, final_stat, col=False)


def kernel(**inputs):
    import concourse.bacc as bacc
    from concourse.bass_utils import run_bass_kernel_spmd

    def columns(g, chunks):
        g = np.asarray(g)
        g = g.reshape(g.shape[:-1] + (chunks, P))
        return np.moveaxis(g, -1, 0)

    per_layer = np.concatenate(
        [columns(inputs[n], c) for n, c in (("norm_mix", DC), ("norm_xattn", DC), ("norm_mem", DC), ("norm_ffn", DC),
                                            ("q_lat_norm", QL // P), ("kv_lat_norm", KL // P))], axis=2)
    gains = np.concatenate([per_layer.reshape(P, DEPTH * GAINS), columns(inputs["norm_final"], DC)], axis=1)
    freq = np.concatenate([np.exp(np.float32(-math.log(THETA) * (2.0 / d)) * np.arange(d // 2, dtype=np.float32))
                           for d in (DA, ROPE)]).astype(np.float32)
    arrays = {
        "xT": np.asarray(inputs["x"])[0].T, "memT": np.asarray(inputs["mem"])[0].T,
        "positions": np.asarray(inputs["positions"]).reshape(TT, P).T, "freqs": np.tile(freq, (P, 1)), "gains": gains,
    }
    for n in ("w_in", "w_uq", "w_ukv", "w_branch_a", "w_branch_b", "w_out", "w_xq", "w_xkv", "w_xo", "w_gate_up",
              "w_down"):
        arrays[n] = np.asarray(inputs[n])
    arrays = {n: np.ascontiguousarray(a) for n, a in arrays.items()}
    nc = bacc.Bacc("TRN2", target_bir_lowering=False, num_devices=1)
    args = [nc.dram_tensor(n, a.shape, mybir.dt.from_np(a.dtype), kind="ExternalInput").ap()
            for n, a in arrays.items()]
    out = nc.dram_tensor("outT", (D, T), F32, kind="ExternalOutput").ap()
    trunk(nc, *args, out)
    r = run_bass_kernel_spmd(nc, [arrays], core_ids=[0])
    return np.ascontiguousarray(r.results[0]["outT"].T)[None]
```

```python
from contextlib import ExitStack
import math

import numpy as np
import concourse.bass as bass
from concourse import mybir

F32 = mybir.dt.float32
F32R = mybir.dt.float32r
BF16 = mybir.dt.bfloat16
I32 = mybir.dt.int32
ALU = mybir.AluOpType
ACT = mybir.ActivationFunctionType
AX = mybir.AxisListType

P = 128
D = 1024
T = 256
TT = T // P
DEPTH = 2
DC = D // P
EPS = 1e-6
THETA = 10000.0
HA, DA = 8, 64
HB, NOPE, ROPE, VB = 8, 64, 32, 64
DB = NOPE + ROPE
QL, KL = 384, 256
LAT = QL + KL + ROPE
ZC = (QL + KL) // P
HX, DX = 4, 128
FF = 2816
FS = 256
NSLICE = FF // FS
HEADS = HA + HB
ALL_HEADS = HEADS + HX
SCALE_A = DA ** -0.5
SCALE_B = DB ** -0.5
SCALE_X = DX ** -0.5
MASKED = -1e30
Z_BANK = (6, 7, 0, 1, 2)
SPLIT = 2048

T_Q, T_K, T_LAT, T_V, T_UQ, T_UKV, T_GATE = 0, 2, 4, 7, 9, 11, 12
T_XK, T_BRANCH, T_OUT, T_XQ, T_XV, T_XO, T_FFN = 20, 22, 26, 30, 32, 34, 36
T_LOOP = T_FFN + 5
LOOPS = NSLICE - 3
T_END = T_LOOP + 3 * LOOPS
T_LAST = T_END + 3
TILES = T_LAST + 1
SLOTS = 3
assert TILES % SLOTS == 0 and T_LOOP % SLOTS == 2

G_MIX, G_X, G_MEM, G_FFN, G_LAT = 0, DC, 2 * DC, 3 * DC, 4 * DC
GAINS = G_LAT + ZC

TURNS = HA // 2 + HB
TURN = []
_rest = 2 * math.pi
for _ in range(3):
    _part = math.ldexp(math.floor(math.ldexp(_rest, 8 - math.frexp(_rest)[1])), math.frexp(_rest)[1] - 8)
    TURN.append(_part)
    _rest -= _part
TURN.append(_rest)
ROUND = 1.5 * 2.0 ** 23
PI_LOW = float(np.nextafter(np.float32(math.pi), np.float32(0)))


def tile_cut(n):
    if n in (T_LAT, T_LAT + 1):
        return 3, LAT
    if n == T_LAT + 2:
        return 2, LAT
    if T_UQ <= n < T_UKV:
        return 3, 384
    if n == T_UKV:
        return 2, 1024
    if n < T_UQ or T_BRANCH <= n < T_OUT or T_XV <= n < T_FFN:
        return 4, 512
    if n in (T_FFN + 4, T_LAST - 1, T_LAST):
        return 2, D
    return 8, 256


def turn_of(s):
    return s // 2 if s < HA else s - HA // 2


def last_head(u):
    return 2 * u + 1 if u < HA // 2 else u + HA // 2


class Steps:

    def __init__(self, eng, sem):
        self.eng, self.sem, self.base, self.n = eng, sem, 0, 0

    def start(self, base):
        self.base, self.n = base, 0

    def done(self, ins):
        self.n += 1
        ins.then_inc(self.sem, 1)
        self.eng.wait_ge(self.sem, self.base + self.n)


def rstd_seed(V, step, y, src, v):
    step.done(V.tensor_scalar(v, src, EPS, None, ALU.add))
    return V.tensor_scalar(y.bitcast(I32), v.bitcast(I32), -0.5, float(0x5F3759DF), ALU.mult, ALU.add)


def rstd_vector(V, step, y, src, work):
    n = src.shape[-1]
    v, t = work[:, 0:n], work[:, n:2 * n]
    step.done(rstd_seed(V, step, y, src, v))
    for i in range(3):
        step.done(V.tensor_tensor(t, y, y, ALU.mult))
        step.done(V.scalar_tensor_tensor(out=t, in0=t, scalar=-0.5, in1=v, op0=ALU.mult, op1=ALU.mult))
        last = V.scalar_tensor_tensor(out=y, in0=t, scalar=1.5, in1=y, op0=ALU.add, op1=ALU.mult)
        if i < 2:
            step.done(last)
    return last


def newton_pool(G, step, y, v, t, constants):
    minus_half, three_halves = (constants[:, i:i + 1].broadcast_to([P, v.shape[-1]]) for i in range(2))
    for i in range(3):
        step.done(G.tensor_tensor(t, y, y, ALU.mult))
        step.done(G.tensor_tensor(t, t, v, ALU.mult))
        step.done(G.tensor_tensor(t, t, minus_half, ALU.mult))
        step.done(G.tensor_tensor(t, t, three_halves, ALU.add))
        last = G.tensor_tensor(y, y, t, ALU.mult)
        if i < 2:
            step.done(last)
    return last


def trunk(nc, xT, memT, positions, gains, w_in, w_uq, w_ukv, w_branch_a, w_branch_b, w_out,
          w_xq, w_xkv, w_xo, w_gate_up, w_down, out):
    with ExitStack() as ctx:
        def sb(name, shape, dt=F32):
            return ctx.enter_context(nc.sbuf_tensor(name, shape, dt))

        def sem(name):
            return ctx.enter_context(nc.semaphore(name))

        raw = [sb(f"raw{i}", [P, SPLIT]) for i in range(SLOTS)]
        w_hi = [sb(f"w_hi{i}", [P, SPLIT], F32R) for i in range(SLOTS)]
        w_lo = [sb(f"w_lo{i}", [P, SPLIT], F32R) for i in range(SLOTS)]
        x = sb("x", [P, DC, T])
        h_hi = sb("h_hi", [P, DC, T], F32R)
        h_lo = sb("h_lo", [P, DC, T], F32R)
        mem = sb("mem", [P, DC, T])
        m_hi = sb("m_hi", [P, DC, T], F32R)
        m_lo = sb("m_lo", [P, DC, T], F32R)
        a_hi = m_hi[:, 0:2, :]
        a_lo = m_lo[:, 0:2, :]
        a_hi_last = m_hi[:, 2:4, :]
        a_lo_last = m_lo[:, 2:4, :]
        q_a = sb("q_a", [P, TT, HA * DA])
        k_a = sb("k_a", [P, TT, HA * DA])
        v_a = sb("v_a", [P, TT, HA * DA])
        q_b = sb("q_b", [P, TT, HB, DB])
        k_b = sb("k_b", [P, TT, HB, DB])
        v_b = sb("v_b", [P, TT, HB, VB])
        xq = q_a[:, :, :].rearrange("p t n -> p (t n)").rearrange("p (h t) -> p h t", t=T)
        xk = k_a[:, :, :].rearrange("p t n -> p (t n)").rearrange("p (h t) -> p h t", t=T)
        xv = v_a
        oz = sb("oz", [P, 2, 8, T], F32R)
        z_hi, z_lo = oz[:, 0, 0:ZC, :], oz[:, 1, 0:ZC, :]
        o_hi, o_lo = oz[:, 0, :, :], oz[:, 1, :, :]
        region = sb("region", [P, 16, T])
        flat = region[:, :, :].rearrange("p a b -> p (a b)")
        z = flat[:, 0:TT * LAT].rearrange("p (t n) -> p t n", t=TT)
        z_sq = flat[:, TT * LAT:TT * LAT + TT * (QL + KL)].rearrange("p (t n) -> p t n", t=TT)
        free = TT * LAT + TT * (QL + KL)
        mem_sum = flat[:, free:free + T]
        mem_temp = flat[:, free + T:free + T + 1024].rearrange("p (a b) -> p a b", a=2)
        mem_v, mem_t = (flat[:, a:a + T + TT] for a in (free + T, free + 2 * T + TT))
        gate = region
        xp = [region[:, 2 * j:2 * j + 2, :] for j in range(HX)]
        xpt = [region[:, 8 + 2 * j:10 + 2 * j, :] for j in range(2)]
        ff_g, ff_t, ff_m = (region[:, 2 * j:2 * j + 2, :] for j in range(3))
        x_gain = region[:, 0:8, :]
        y = flat[:, 8 * T:16 * T].rearrange("p (t n) -> p t n", t=TT)
        temp = sb("temp", [P, 4, 512])
        square_sum = sb("square_sum", [P, T])
        qk_t = [sb(f"qk_t{i}", [P, 4 * P]) for i in range(2)]
        prob = [sb(f"prob{i}", [P, 3 * P]) for i in range(2)]
        prob_t = [sb(f"prob_t{i}", [P, 3 * P]) for i in range(2)]
        row_max = [sb(f"row_max{i}", [P, TT]) for i in range(4)]
        bias = [sb(f"bias{i}", [P, TT]) for i in range(4)]
        row_sum = [sb(f"row_sum{i}", [P, TT]) for i in range(4)]
        row_inv = [sb(f"row_inv{i}", [P, TT]) for i in range(4)]
        rstd_both = sb("rstd_both", [P, T + TT])
        rstd_row = rstd_both[:, 0:T]
        rstd_col = rstd_both[:, T:T + TT]
        mem_rstd = sb("mem_rstd", [P, T + TT])
        mem_row, mem_col = mem_rstd[:, 0:T], mem_rstd[:, T:T + TT]
        x_scale = sb("x_scale", [P, TT])
        lat_ms = sb("lat_ms", [P, TT, 2])
        lat_rstd = sb("lat_rstd", [P, TT, 2])
        gain_all = sb("gain_all", [P, (DEPTH + 1) * GAINS + 48])
        freq = gain_all[:, (DEPTH + 1) * GAINS:]
        gain = sb("gain", [P, GAINS])
        pos_i = sb("pos_i", [P, TT], I32)
        pos_f = sb("pos_f", [P, TT])
        angle, turns, trig = (q_b[:, :, :, :].rearrange("p t h n -> p (t h n)")[:, 192 * i:192 * i + 192]
                              .rearrange("p (f t n) -> p f t n", f=2, t=TT) for i in range(3))
        cos_a, sin_a = sb("cos_a", [P, TT, 64]), sb("sin_a", [P, TT, 64])
        cos_b, sin_b = sb("cos_b", [P, TT, 32]), sb("sin_b", [P, TT, 32])
        cos_ar, sin_ar = sb("cos_ar", [P, TT, 64]), sb("sin_ar", [P, TT, 64])
        cos_br, sin_br = sb("cos_br", [P, TT, 32]), sb("sin_br", [P, TT, 32])
        ident = sb("ident", [P, P])
        ident_h = sb("ident_h", [P, P], BF16)
        mask = sb("mask", [P, P], BF16)
        mean_of = sb("mean_of", [P, P])
        newton = sb("newton", [P, 2])

        ps = ctx.enter_context(nc.psum_tensor("ps", [P, 8, 512], F32))

        raw_landed = [sem(f"raw_landed{i}") for i in range(SLOTS)]
        w_hi_done = sem("w_hi_done")
        w_lo_done = sem("w_lo_done")
        tile_used = sem("tile_used")
        x_loaded = sem("x_loaded")
        mem_loaded = sem("mem_loaded")
        const_loaded = sem("const_loaded")
        consts_made = sem("consts_made")
        x_ready = sem("x_ready")
        h_hi_done = sem("h_hi_done")
        h_lo_done = sem("h_lo_done")
        pair_done = sem("pair_done")
        sums_ready = sem("sums_ready")
        stat_done = sem("stat_done")
        rstd_ready = sem("rstd_ready")
        gains_ready = sem("gains_ready")
        rope_mul = sem("rope_mul")
        rope_sum = sem("rope_sum")
        mem_seeded = sem("mem_seeded")
        mem_rstd_ready = sem("mem_rstd_ready")
        lat_copied = sem("lat_copied")
        lat_squared = sem("lat_squared")
        lat_rstd_ready = sem("lat_rstd_ready")
        kpe_mul = sem("kpe_mul")
        kpe_sum = sem("kpe_sum")
        z_turned = sem("z_turned")
        z_hi_done = sem("z_hi_done")
        z_lo_done = sem("z_lo_done")
        v_copied = sem("v_copied")
        qb_copied = sem("qb_copied")
        qb_mul = sem("qb_mul")
        qb_sum = sem("qb_sum")
        kb_copied = sem("kb_copied")
        vb_copied = sem("vb_copied")
        head_turned = sem("head_turned")
        head_copied = sem("head_copied")
        scored = sem("scored")
        max_ready = sem("max_ready")
        exp_done = sem("exp_done")
        prob_ready = sem("prob_ready")
        prob_turned = sem("prob_turned")
        prob_copied = sem("prob_copied")
        attended = sem("attended")
        o_hi_done = sem("o_hi_done")
        o_lo_done = sem("o_lo_done")
        gate_scaled = sem("gate_scaled")
        gate_tanh = sem("gate_tanh")
        m_hi_done = sem("m_hi_done")
        m_lo_done = sem("m_lo_done")
        xk_copied = sem("xk_copied")
        branch_half = sem("branch_half")
        merge_ready = sem("merge_ready")
        merge_hi = sem("merge_hi")
        merge_lo = sem("merge_lo")
        xq_copied = sem("xq_copied")
        xv_copied = sem("xv_copied")
        g_scaled = sem("g_scaled")
        g_tanh = sem("g_tanh")
        hidden_gated = sem("hidden_gated")
        hidden_ready = sem("hidden_ready")
        a_hi_done = sem("a_hi_done")
        a_lo_done = sem("a_lo_done")
        final_squared = sem("final_squared")
        final_scaled = sem("final_scaled")
        final_turned = sem("final_turned")
        final_stat = sem("final_stat")
        y_ready = [sem("y_ready_act"), sem("y_ready_dve")]
        stored = sem("stored")
        pool_step = sem("pool_step")
        dve_step = sem("dve_step")
        act_step = sem("act_step")

        DVE_STEPS = 2 + 2 * ALL_HEADS + 4 + 1 + NSLICE + 4 * 10 + 1
        POOL_STEPS = 4 * 7 + 14

        def wide(row, n):
            return row.unsqueeze(1).broadcast_to([P, n, T])

        block = ctx.enter_context(nc.Block())

        @block.sync
        def _(sp):
            def kpn(w):
                return w.rearrange("l (c p) n -> l p c n", p=P)

            in_v, uq_v, ukv_v = kpn(w_in), kpn(w_uq), kpn(w_ukv)
            ba_v, bb_v, out_v = kpn(w_branch_a), kpn(w_branch_b), kpn(w_out)
            xq_v, xkv_v, xo_v = kpn(w_xq), kpn(w_xkv), kpn(w_xo)
            gu_v, down_v = kpn(w_gate_up), kpn(w_down)
            half = HX * DX

            def source(n):
                lat0 = 3 * HA * DA
                gate0 = lat0 + LAT
                if n < T_K:
                    return in_v, 4 * (n - T_Q), 0
                if n < T_LAT:
                    return in_v, 4 * (n - T_K), HA * DA
                if n < T_V:
                    return in_v, 3 * (n - T_LAT), lat0
                if n < T_UQ:
                    return in_v, 4 * (n - T_V), 2 * HA * DA
                if n < T_UKV:
                    return uq_v, 0, 384 * (n - T_UQ)
                if n < T_GATE:
                    return ukv_v, 0, 0
                if n < T_XK:
                    return in_v, 0, gate0 + 256 * (n - T_GATE)
                if n < T_BRANCH:
                    return xkv_v, 0, 256 * (n - T_XK)
                if n < T_OUT:
                    return (ba_v, bb_v)[(n - T_BRANCH) % 2], 0, 512 * ((n - T_BRANCH) // 2)
                if n < T_XQ:
                    return out_v, 0, 256 * (n - T_OUT)
                if n < T_XV:
                    return xq_v, 0, 256 * (n - T_XQ)
                if n < T_XO:
                    return xkv_v, 4 * (n - T_XV), half
                if n < T_FFN:
                    return xo_v, 0, 512 * (n - T_XO)
                return {T_FFN: (gu_v, 0, 0), T_FFN + 1: (gu_v, 0, FF), T_FFN + 2: (gu_v, 0, FS),
                        T_FFN + 3: (gu_v, 0, FF + FS), T_FFN + 4: (down_v, 0, 0),
                        T_END: (gu_v, 0, FS * (NSLICE - 1)), T_END + 1: (gu_v, 0, FF + FS * (NSLICE - 1)),
                        T_END + 2: (down_v, 2 * (NSLICE - 2), 0), T_LAST: (down_v, 2 * (NSLICE - 1), 0)}[n]

            def load(l, n):
                w, c0, col = source(n)
                c, m = tile_cut(n)
                dst = raw[n % SLOTS][:, 0:c * m].rearrange("p (c n) -> p c n", c=c)
                sp.dma_start(dst, w[l, :, c0:c0 + c, col:col + m]).then_inc(raw_landed[n % SLOTS], 16)

            sp.dma_start(pos_i[:, :], positions).then_inc(const_loaded, 16)
            load(0, 0)
            sp.dma_start(x[:, :, :], xT.rearrange("(c p) t -> p c t", p=P)).then_inc(x_loaded, 16)
            load(0, 1)
            load(0, 2)
            with_slots = [raw[i][:, :] for i in range(SLOTS)]
            with sp.Fori(0, DEPTH) as l:
                for n in range(T_LOOP - SLOTS):
                    sp.wait_ge(w_lo_done, l * TILES + n + 1)
                    load(l, n + SLOTS)
                with sp.Fori(0, LOOPS) as k:
                    for j in range(3):
                        sp.wait_ge(w_lo_done, l * TILES + k * 3 + (T_LOOP - SLOTS + j + 1))
                        slot = (T_LOOP + j) % SLOTS
                        if j == 1:
                            src = down_v[l, :, bass.ds(k * 2 + 2, 2), :]
                            dst = with_slots[slot].rearrange("p (c n) -> p c n", c=2)
                        else:
                            src = gu_v[l, :, :, bass.ds(k * FS + (2 * FS + (FF if j else 0)), FS)]
                            dst = with_slots[slot].rearrange("p (c n) -> p c n", c=8)
                        sp.dma_start(dst, src).then_inc(raw_landed[slot], 16)
                for n in range(T_END, TILES):
                    sp.wait_ge(w_lo_done, l * TILES + n - SLOTS + 1)
                    load(l, n)
                following = (l + 1) % DEPTH
                for n in range(SLOTS):
                    sp.wait_ge(w_lo_done, l * TILES + T_LAST - 1 + n)
                    load(following, n)
            for j in range(4):
                t, half = divmod(j, 2)
                sp.wait_ge(y_ready[half], t + 1)
                sp.dma_start(out[t * P:t * P + P, 512 * half:512 * half + 512],
                             y[:, t, 512 * half:512 * half + 512]).then_inc(stored, 16)
            for i in range(SLOTS):
                sp.wait_ge(raw_landed[i], 16 * (DEPTH * (TILES // SLOTS) + 1))
            sp.wait_ge(stored, 64)

        @block.gpsimd
        def _(pool):
            step = Steps(pool, pool_step)
            nc.gpsimd.memset(mean_of[:, :], 1.0 / D)
            for i, value in enumerate((-0.5, 1.5)):
                nc.gpsimd.memset(newton[:, i:i + 1], value)
            nc.gpsimd.memset(ident[:, :], 0.0)
            nc.gpsimd.memset(ident_h[:, :], 0.0)
            step.done(nc.gpsimd.memset(mask[:, :], 0.0))
            for m in (ident, ident_h):
                nc.gpsimd.affine_select(out=m[:, :], in_=m[:, :], compare_op=ALU.not_equal, fill=1.0, base=0,
                                        pattern=[[-1, P]], channel_multiplier=1)
            nc.gpsimd.affine_select(out=mask[:, :], in_=mask[:, :], compare_op=ALU.is_ge, fill=MASKED, base=0,
                                    pattern=[[-1, P]], channel_multiplier=1).then_inc(consts_made, 1)

            def add_squares(src, ready, done, temp=temp, square_sum=square_sum):
                for p in range(4):
                    ready(p)
                    pair = src[:, 2 * p:2 * p + 2, :].rearrange("p c t -> p (c t)")
                    part = temp[:, min(p, 1), :]
                    step.done(nc.gpsimd.tensor_tensor(part, pair, pair, ALU.mult))
                    if p:
                        last = nc.gpsimd.tensor_tensor(temp[:, 0, :], temp[:, 0, :], part, ALU.add)
                        step.done(last)
                nc.gpsimd.tensor_tensor(square_sum[:, :], temp[:, 0, 0:T], temp[:, 0, T:2 * T],
                                        ALU.add).then_inc(done, 1)

            pool.wait_ge(x_loaded, 16)
            pool.sem_inc(x_ready, 4)
            start = step.n
            with pool.Fori(0, DEPTH) as l:
                step.start(l * POOL_STEPS + start)
                add_squares(x, lambda p: pool.wait_ge(x_ready, l * 12 + p + 1), sums_ready)
                add_squares(mem, lambda p: pool.wait_ge(mem_loaded, 16), sums_ready, mem_temp, mem_sum)
                for i in range(4):
                    pool.wait_ge(rope_mul, l * 4 + i + 1)
                    out = (q_a, k_a)[i // 2][:, i % 2, :]
                    a = temp[:, 2 * (i % 2), :]
                    b = temp[:, 2 * (i % 2) + 1, :]
                    nc.gpsimd.tensor_tensor(out, a, b, ALU.add).then_inc(rope_sum, 1)
                pool.wait_ge(kpe_mul, l + 1)
                ka = temp[:, 0, 0:64].rearrange("p (t n) -> p t n", t=TT)
                kb = temp[:, 0, 64:128].rearrange("p (t n) -> p t n", t=TT)
                for t in range(TT):
                    last = nc.gpsimd.tensor_tensor(k_b[:, t, :, NOPE:DB],
                                                   ka[:, t, :].unsqueeze(1).broadcast_to([P, HB, ROPE]),
                                                   kb[:, t, :].unsqueeze(1).broadcast_to([P, HB, ROPE]), ALU.add)
                last.then_inc(kpe_sum, 1)
                for i in range(4):
                    pool.wait_ge(qb_mul, l * 4 + i + 1)
                    half, t = divmod(i, 2)
                    a = temp[:, 1 + i // 2, 256 * (i % 2):256 * (i % 2) + 128].rearrange("p (h n) -> p h n", h=4)
                    b = temp[:, 1 + i // 2, 256 * (i % 2) + 128:256 * (i % 2) + 256]\
                        .rearrange("p (h n) -> p h n", h=4)
                    nc.gpsimd.tensor_tensor(q_b[:, t, 4 * half:4 * half + 4, NOPE:DB], a, b,
                                            ALU.add).then_inc(qb_sum, 1)
                def low(n):
                    pool.wait_ge(w_hi_done, l * TILES + n + 1)
                    pool.wait_ge(w_lo_done, l * TILES + n)
                    c, m = tile_cut(n)
                    nc.gpsimd.tensor_tensor(w_lo[n % SLOTS][:, 0:c * m], raw[n % SLOTS][:, 0:c * m],
                                            w_hi[n % SLOTS][:, 0:c * m].bitcast(F32),
                                            ALU.subtract).then_inc(w_lo_done, 1)

                low(T_GATE + 1)
                pool.wait_ge(mem_seeded, l + 1)
                newton_pool(nc.gpsimd, step, mem_rstd[:, :], mem_v, mem_t, newton).then_inc(mem_rstd_ready, 1)
                for n in range(T_GATE + 2, T_XK + 2):
                    low(n)
                low(T_OUT + 1)
                add_squares(x, lambda p: pool.wait_ge(x_ready, l * 12 + 4 + p + 1), sums_ready)
                add_squares(x, lambda p: pool.wait_ge(x_ready, l * 12 + 8 + p + 1), sums_ready)
            assert step.n == POOL_STEPS, step.n

        @block.scalar
        def _(act):
            act.dma_start(gain_all[:, :], gains).then_inc(const_loaded, 16)

            def split(l, n):
                act.wait_ge(raw_landed[n % SLOTS], (l * (TILES // SLOTS) + n // SLOTS + 1) * 16)
                if n >= SLOTS:
                    act.wait_ge(tile_used, l * TILES + (n - SLOTS + 2))
                elif n == 2:
                    act.wait_ge(tile_used, l * TILES + 1)
                c, m = tile_cut(n % TILES)
                nc.scalar.activation(w_hi[n % SLOTS][:, 0:c * m], raw[n % SLOTS][:, 0:c * m],
                                     ACT.Copy).then_inc(w_hi_done, 1)

            act.wait_ge(act_step, 1)
            nc.scalar.activation(trig[:, :, :, :], angle[:, :, :, :], ACT.Sin).then_inc(act_step, 1)
            act.wait_ge(raw_landed[0], 16)
            for part, done in ((slice(0, SPLIT // 2), act_step), (slice(SPLIT // 2, SPLIT), w_hi_done)):
                nc.scalar.activation(w_hi[0][:, part], raw[0][:, part], ACT.Copy).then_inc(done, 1)
            act.dma_start(mem[:, :, :], memT.rearrange("(c p) t -> p c t", p=P)).then_inc(mem_loaded, 16)

            def used(l, n):
                act.wait_ge(tile_used, l * TILES + n + 2)

            def h_split(l, norm, chunks, g0, h_hi=h_hi):
                for c in chunks:
                    if c % 2 == 0:
                        act.wait_ge(x_ready, l * 12 + 4 * norm + c // 2 + 1)
                    nc.scalar.activation(h_hi[:, c, :], x[:, c, :], ACT.Copy,
                                         scale=gain[:, g0 + c:g0 + c + 1]).then_inc(h_hi_done, 1)

            def head_copy(l, u):
                d = P if u < HA // 2 else DB
                act.wait_ge(head_turned, l * TURNS + u + 1)
                if u >= 2:
                    act.wait_ge(scored, l * ALL_HEADS + last_head(u - 2) + 1)
                nc.scalar.activation(qk_t[u % 2][0:d, :], ps[0:d, 5, :], ACT.Copy).then_inc(head_copied, 1)

            def head_exp(l, s):
                scale = SCALE_A if s < HA else SCALE_B
                act.wait_ge(max_ready, l * ALL_HEADS + s + 1)
                if s >= 2:
                    act.wait_ge(prob_turned, l * ALL_HEADS + s - 1)
                for t in range(TT):
                    cols = slice(0, P) if t == 0 else slice(P, 3 * P)
                    last = nc.scalar.activation(prob[s % 2][:, cols], ps[:, 6 + s % 2, cols], ACT.Exp,
                                                bias=bias[s % 2][:, t:t + 1], scale=scale,
                                                accum_out=row_sum[s % 2][:, t:t + 1])
                last.then_inc(exp_done, 1)

            def o_pair(l, r):
                act.wait_ge(attended, l * ALL_HEADS + 2 * r + 2)
                nc.scalar.activation(o_hi[:, r, :], ps[:, r % 2, 0:T], ACT.Copy).then_inc(o_hi_done, 1)

            def merge_split(l, p):
                act.wait_ge(merge_ready, l * 4 + p + 1)
                nc.scalar.activation(h_hi[:, 2 * p:2 * p + 2, :], gate[:, 2 * p:2 * p + 2, :],
                                     ACT.Copy).then_inc(merge_hi, 1)

            def hidden_tanh(i):
                act.wait_ge(g_scaled, i + 1)
                nc.scalar.activation(ff_t, ff_g, ACT.Tanh, scale=0.5).then_inc(g_tanh, 1)

            def hidden_split(i, dst=a_hi):
                act.wait_ge(hidden_ready, i + 1)
                nc.scalar.activation(dst, ff_m, ACT.Copy).then_inc(a_hi_done, 1)

            with act.Fori(0, DEPTH) as l:
                act.wait_ge(gains_ready, l + 1)
                h_split(l, 0, range(DC), G_MIX)
                split(l, 1)
                for n in range(T_LAT + 3):
                    split(l, n + 2)
                used(l, T_LAT + 2)
                act.wait_ge(rstd_ready, l * 3 + 1)
                for t in range(TT):
                    for i in range(2):
                        nc.scalar.activation(z[:, t, 336 * i:336 * i + 336], ps[:, 2 * t + i, 0:336], ACT.Copy,
                                             scale=rstd_col[:, t:t + 1]).then_inc(lat_copied, 1)
                split(l, T_V + 2)
                act.wait_ge(lat_copied, l * 4 + 4)
                for t in range(TT):
                    for i, (a, b) in enumerate(((0, QL), (QL, QL + KL))):
                        nc.scalar.activation(z_sq[:, t, a:b], z[:, t, a:b], ACT.Square, scale=(b - a) ** -0.5,
                                             accum_out=lat_ms[:, t, i:i + 1]).then_inc(lat_squared, 1)
                for c in range(ZC):
                    act.wait_ge(z_turned, l * ZC + c + 1)
                    b = Z_BANK[c]
                    nc.scalar.activation(z_hi[:, c, :], ps[:, b, 0:T], ACT.Copy,
                                         scale=gain[:, G_LAT + c:G_LAT + c + 1]).then_inc(z_hi_done, 1)
                split(l, T_V + 3)
                used(l, T_V + 1)
                for t in range(TT):
                    nc.scalar.activation(v_a[:, t, :], ps[:, 4 + t, :], ACT.Copy,
                                         scale=rstd_col[:, t:t + 1]).then_inc(v_copied, 1)
                split(l, T_UQ + 2)
                act.wait_ge(lat_rstd_ready, l + 1)
                for i in range(2):
                    used(l, T_UQ + i)
                    for t in range(TT):
                        src = ps[:, 2 + 2 * i + t, 0:384].rearrange("p (h n) -> p h n", h=4)
                        nc.scalar.activation(q_b[:, t, 4 * i:4 * i + 4, 0:NOPE], src[:, :, 0:NOPE], ACT.Copy,
                                             scale=lat_rstd[:, t, 0:1]).then_inc(qb_copied, 1)
                    split(l, T_UQ + 3 + i)
                used(l, T_UKV)
                for t in (1, 0):
                    for i in range(2):
                        if t == 0:
                            act.wait_ge(vb_copied, l * 4 + i + 1)
                        src = ps[:, 6 * t + i, :].rearrange("p (h n) -> p h n", h=4)
                        nc.scalar.activation(k_b[:, t, 4 * i:4 * i + 4, 0:NOPE], src[:, :, 0:NOPE], ACT.Copy,
                                             scale=lat_rstd[:, t, 1:2]).then_inc(kb_copied, 1)
                    if t == 1:
                        head_copy(l, 0)
                for s in range(HEADS):
                    g = s // 2
                    if s + 1 < HEADS and turn_of(s + 1) != turn_of(s):
                        head_copy(l, turn_of(s + 1))
                    head_exp(l, s)
                    if s % 2 == 0:
                        if g >= 1:
                            o_pair(l, g - 1)
                            act.wait_ge(gate_scaled, l * 8 + g)
                            tile = gate[:, 2 * g - 2:2 * g, :]
                            nc.scalar.activation(tile, tile, ACT.Tanh, scale=0.5).then_inc(gate_tanh, 1)
                        split(l, T_GATE + 2 + g)
                    else:
                        if g == 0:
                            used(l, T_GATE - 1)
                        nc.scalar.activation(m_hi[:, g, :], mem[:, g, :], ACT.Copy,
                                             scale=gain[:, G_MEM + g:G_MEM + g + 1]).then_inc(m_hi_done, 1)
                act.wait_ge(gate_scaled, l * 8 + 8)
                nc.scalar.activation(gate[:, 14:16, :], gate[:, 14:16, :], ACT.Tanh, scale=0.5).then_inc(gate_tanh, 1)
                split(l, T_XK + 2)
                o_pair(l, HEADS // 2 - 1)
                split(l, T_XK + 3)
                split(l, T_BRANCH + 2)
                split(l, T_BRANCH + 3)
                merge_split(l, 0)
                merge_split(l, 1)
                split(l, T_BRANCH + 4)
                split(l, T_BRANCH + 5)
                merge_split(l, 2)
                merge_split(l, 3)
                split(l, T_OUT + 2)
                for j in range(4):
                    if j < 3:
                        split(l, T_OUT + 3 + j)
                    h_split(l, 1, (2 * j, 2 * j + 1), G_X, o_hi)
                split(l, T_XQ + 2)
                for j in range(2):
                    used(l, T_XQ + j)
                    b = 4 + 2 * j
                    nc.scalar.activation(xq[:, 2 * j:2 * j + 2, :], ps[:, b:b + 2, 0:T],
                                         ACT.Copy).then_inc(xq_copied, 1)
                    if j == 0:
                        split(l, T_XQ + 3)
                for j in range(HX):
                    s = HEADS + j
                    act.wait_ge(max_ready, l * ALL_HEADS + s + 1)
                    for t in range(TT):
                        last = nc.scalar.activation(xp[j][:, t, :], ps[:, j, T * t:T * t + T], ACT.Exp,
                                                    bias=bias[j][:, t:t + 1], scale=x_scale[:, t:t + 1],
                                                    accum_out=row_sum[j][:, t:t + 1])
                    last.then_inc(exp_done, 1)
                    if j == 1:
                        split(l, T_XV + 2)
                split(l, T_XV + 3)
                used(l, T_XV + 1)
                nc.scalar.activation(xv[:, 0, :], ps[:, 6, :], ACT.Copy,
                                     scale=mem_col[:, 0:1]).then_inc(xv_copied, 1)
                split(l, T_XO + 2)
                for r in range(2):
                    act.wait_ge(attended, l * ALL_HEADS + HEADS + 2 * r + 2)
                    nc.scalar.activation(o_hi[:, 2 * r:2 * r + 2, :],
                                         ps[:, 4 + r, :].rearrange("p (h t) -> p h t", h=2),
                                         ACT.Copy).then_inc(o_hi_done, 1)
                h_split(l, 2, range(4), G_FFN)
                split(l, T_XO + 3)
                h_split(l, 2, range(4, DC), G_FFN)
                split(l, T_FFN + 2)
                split(l, T_FFN + 3)
                split(l, T_FFN + 4)
                hidden_tanh(l * NSLICE)
                hidden_split(l * NSLICE)
                hidden_tanh(l * NSLICE + 1)
                split(l, T_FFN + 5)
                split(l, T_FFN + 6)
                with act.Fori(0, LOOPS) as k:
                    def loop_split(j):
                        slot = (T_LOOP + 2 + j) % SLOTS
                        n = T_LOOP + 2 + j
                        act.wait_ge(raw_landed[slot], (l * (TILES // SLOTS) + k + (n // SLOTS + 1)) * 16)
                        act.wait_ge(tile_used, l * TILES + k * 3 + (n - SLOTS + 2))
                        nc.scalar.activation(w_hi[slot][:, :], raw[slot][:, :], ACT.Copy).then_inc(w_hi_done, 1)
                    hidden_split(l * NSLICE + k + 1)
                    loop_split(0)
                    hidden_tanh(l * NSLICE + k + 2)
                    loop_split(1)
                    loop_split(2)
                hidden_split(l * NSLICE + (NSLICE - 2))
                split(l, T_END + 2)
                hidden_tanh(l * NSLICE + (NSLICE - 1))
                split(l, T_END + 3)
                hidden_split(l * NSLICE + (NSLICE - 1), a_hi_last)
                split(l, TILES)
            for p in range(4):
                act.wait_ge(x_ready, DEPTH * 12 + p + 1)
                nc.scalar.activation(temp[:, p, :].rearrange("p (c t) -> p c t", c=2), x[:, 2 * p:2 * p + 2, :],
                                     ACT.Square).then_inc(final_squared, 1)
            act.wait_ge(final_stat, 2)
            for t in range(TT):
                act.wait_ge(final_turned, t + 1)
                nc.scalar.activation(y[:, t, 0:512], ps[:, 4 + 2 * t, :], ACT.Copy,
                                     scale=rstd_col[:, t:t + 1]).then_inc(y_ready[0], 1)

        @block.vector
        def _(dve):
            step = Steps(dve, dve_step)
            V = nc.vector

            def split(l, n):
                dve.wait_ge(w_hi_done, l * TILES + n + 1)
                c, m = tile_cut(n % TILES)
                V.tensor_tensor(w_lo[n % SLOTS][:, 0:c * m], raw[n % SLOTS][:, 0:c * m],
                                w_hi[n % SLOTS][:, 0:c * m].bitcast(F32), ALU.subtract).then_inc(w_lo_done, 1)

            def split_half(l, n, i):
                c, m = tile_cut(n)
                part = slice(i * c * m // 2, (i + 1) * c * m // 2)
                ins = V.tensor_tensor(w_lo[n % SLOTS][:, part], raw[n % SLOTS][:, part],
                                      w_hi[n % SLOTS][:, part].bitcast(F32), ALU.subtract)
                if i == 1:
                    ins.then_inc(w_lo_done, 1)

            dve.wait_ge(const_loaded, 32)
            V.tensor_copy(gain[:, :], gain_all[:, 0:GAINS]).then_inc(gains_ready, 1)
            step.done(V.tensor_copy(pos_f[:, :], pos_i[:, :]))
            for t in range(TT):
                last = V.tensor_scalar(angle[:, 0, t, :], freq[:, :], pos_f[:, t:t + 1], None, ALU.mult)
            step.done(last)
            ang, cosine, trn = angle[:, 0, :, :], angle[:, 1, :, :], turns[:, 0, :, :]
            step.done(V.tensor_scalar(trn, ang, 1 / (2 * math.pi), ROUND, ALU.mult, ALU.add))
            step.done(V.tensor_scalar(trn, trn, ROUND, None, ALU.subtract))
            for part in TURN:
                step.done(V.scalar_tensor_tensor(out=ang, in0=trn, scalar=-part, in1=ang, op0=ALU.mult, op1=ALU.add))
            step.done(V.tensor_scalar(cosine, ang, math.pi / 2, None, ALU.add))
            step.done(V.tensor_scalar(trn, cosine, math.pi, -2 * math.pi, ALU.is_gt, ALU.mult))
            step.done(V.tensor_tensor(cosine, cosine, trn, ALU.add))
            V.tensor_scalar(angle[:, :, :, :], angle[:, :, :, :], PI_LOW, -PI_LOW, ALU.min,
                            ALU.max).then_inc(act_step, 1)
            dve.wait_ge(act_step, 2)
            for c_t, s_t, f0, m in ((cos_a, sin_a, 0, 32), (cos_b, sin_b, 32, 16)):
                V.tensor_copy(c_t[:, :, 0:m], trig[:, 1, :, f0:f0 + m])
                V.tensor_copy(c_t[:, :, m:2 * m], trig[:, 1, :, f0:f0 + m])
                V.tensor_scalar(s_t[:, :, 0:m], trig[:, 0, :, f0:f0 + m], -1.0, None, ALU.mult)
                last = V.tensor_copy(s_t[:, :, m:2 * m], trig[:, 0, :, f0:f0 + m])
            step.done(last)
            dve.wait_ge(act_step, 3)
            split_half(0, 0, 0)
            dve.wait_ge(w_hi_done, 1)
            split_half(0, 0, 1)

            work = temp[:, 2:4, :].rearrange("p a b -> p (a b)")
            def used(l, n):
                dve.wait_ge(tile_used, l * TILES + n + 2)

            def h_split(l, norm, chunks, g0, h_hi=h_hi, h_lo=h_lo):
                for c in chunks:
                    dve.wait_ge(h_hi_done, l * 24 + 8 * norm + c + 1)
                    V.scalar_tensor_tensor(out=h_lo[:, c, :], in0=x[:, c, :], scalar=gain[:, g0 + c:g0 + c + 1],
                                           in1=h_hi[:, c, :].bitcast(F32), op0=ALU.mult,
                                           op1=ALU.subtract).then_inc(h_lo_done, 1)

            def swapped(ap, m):
                v = ap.rearrange("p (h j n) -> p h j n", j=2, n=m)
                return [v[:, :, 1, :], v[:, :, 0, :]]

            def rope_a(l, i):
                t = i % 2
                src = ps[:, 4 + i, :]
                if i >= 2:
                    dve.wait_ge(rope_sum, l * 4 + i - 1)
                V.tensor_tensor(temp[:, 2 * t, :].rearrange("p (h n) -> p h n", h=HA),
                                src.rearrange("p (h n) -> p h n", h=HA),
                                cos_ar[:, t, :].unsqueeze(1).broadcast_to([P, HA, DA]), ALU.mult)
                other = temp[:, 2 * t + 1, :].rearrange("p (h j n) -> p h j n", j=2, n=32)
                for j, part in enumerate(swapped(src, 32)):
                    last = V.tensor_tensor(other[:, :, j, :], part,
                                           sin_ar[:, t, 32 * j:32 * j + 32].unsqueeze(1).broadcast_to([P, HA, 32]),
                                           ALU.mult)
                last.then_inc(rope_mul, 1)

            def head_max(l, s):
                dve.wait_ge(scored, l * ALL_HEADS + s + 1)
                V.tensor_reduce(row_max[s % 2][:, 0:1], ps[:, 6 + s % 2, 0:P], AX.X, ALU.max)
                step.done(V.tensor_reduce(row_max[s % 2][:, 1:2], ps[:, 6 + s % 2, P:3 * P], AX.X, ALU.max))
                V.tensor_scalar(bias[s % 2][:, :], row_max[s % 2][:, :], -(SCALE_A if s < HA else SCALE_B), None,
                                ALU.mult).then_inc(max_ready, 1)

            def head_norm(l, s):
                dve.wait_ge(exp_done, l * ALL_HEADS + s + 1)
                step.done(V.reciprocal(row_inv[s % 2][:, :], row_sum[s % 2][:, :]))
                V.tensor_scalar(prob[s % 2][:, 0:P], prob[s % 2][:, 0:P], row_inv[s % 2][:, 0:1], None, ALU.mult)
                V.tensor_scalar(prob[s % 2][:, P:3 * P], prob[s % 2][:, P:3 * P], row_inv[s % 2][:, 1:2], None,
                                ALU.mult).then_inc(prob_ready, 1)

            def prob_copy(l, s):
                dve.wait_ge(prob_turned, l * ALL_HEADS + s + 1)
                if s >= 2:
                    dve.wait_ge(attended, l * ALL_HEADS + s - 1)
                V.tensor_copy(prob_t[s % 2][:, :], ps[:, 4, 0:3 * P]).then_inc(prob_copied, 1)

            def o_pair(l, r):
                dve.wait_ge(o_hi_done, l * 10 + r + 1)
                V.tensor_tensor(o_lo[:, r, :], ps[:, r % 2, 0:T], o_hi[:, r, :].bitcast(F32),
                                ALU.subtract).then_inc(o_lo_done, 1)

            def gate_scale(l, g):
                used(l, T_GATE + g)
                V.tensor_tensor(gate[:, 2 * g:2 * g + 2, :], ps[:, 2 + g % 2, :].rearrange("p (c t) -> p c t", c=2),
                                wide(rstd_row[:, :], 2), ALU.mult).then_inc(gate_scaled, 1)

            def banks(b):
                if isinstance(b, tuple):
                    return ps[:, b[0]:b[1] + 1, 0:T]
                return ps[:, b, :].rearrange("p (c t) -> p c t", c=2)

            def add_to_x(pair, b, factor):
                V.scalar_tensor_tensor(out=x[:, 2 * pair:2 * pair + 2, :], in0=banks(b), scalar=factor,
                                       in1=x[:, 2 * pair:2 * pair + 2, :], op0=ALU.mult,
                                       op1=ALU.add).then_inc(x_ready, 1)

            def gated(i, b, p):
                tile = gate[:, 8 * i + 2 * p:8 * i + 2 * p + 2, :]
                return V.scalar_tensor_tensor(out=tile, in0=tile, scalar=1.0, in1=banks(b), op0=ALU.add,
                                              op1=ALU.mult)

            def merge(l, p):
                a, b = gate[:, 2 * p:2 * p + 2, :], gate[:, 8 + 2 * p:10 + 2 * p, :]
                V.tensor_tensor(a, a, b, ALU.add).then_inc(merge_ready, 1)

            def merge_split(l, p):
                dve.wait_ge(merge_hi, l * 4 + p + 1)
                V.tensor_tensor(h_lo[:, 2 * p:2 * p + 2, :], gate[:, 2 * p:2 * p + 2, :],
                                h_hi[:, 2 * p:2 * p + 2, :].bitcast(F32), ALU.subtract).then_inc(merge_lo, 1)

            def hidden_scale(b):
                V.tensor_tensor(ff_g, banks(b), wide(rstd_row[:, :], 2), ALU.mult).then_inc(g_scaled, 1)

            def hidden_gate(i):
                dve.wait_ge(g_tanh, i + 1)
                step.done(V.scalar_tensor_tensor(out=ff_m, in0=ff_t, scalar=1.0, in1=ff_g, op0=ALU.add,
                                                 op1=ALU.mult))
                V.tensor_tensor(ff_m, ff_m, wide(rstd_row[:, :], 2), ALU.mult).then_inc(hidden_gated, 1)

            def hidden_times_up(i, hi=a_hi, lo=a_lo, b=5):
                dve.wait_ge(hidden_gated, i + 1)
                V.tensor_tensor(ff_m, ff_m, banks(b), ALU.mult).then_inc(hidden_ready, 1)
                dve.wait_ge(a_hi_done, i + 1)
                V.tensor_tensor(lo, ff_m, hi.bitcast(F32), ALU.subtract).then_inc(a_lo_done, 1)

            start = step.n
            with dve.Fori(0, DEPTH) as l:
                step.start(l * DVE_STEPS + start)
                dve.wait_ge(gains_ready, l + 1)
                h_split(l, 0, range(DC), G_MIX)
                split(l, 1)
                split(l, 2)
                split(l, 3)
                dve.wait_ge(stat_done, l * 4 + 1)
                rstd_vector(V, step, rstd_both[:, :], ps[:, 0, 0:T + TT], work).then_inc(rstd_ready, 1)
                dve.wait_ge(rstd_ready, l * 3 + 1)
                for t in range(TT):
                    V.tensor_scalar(cos_ar[:, t, :], cos_a[:, t, :], rstd_col[:, t:t + 1], None, ALU.mult)
                    last = V.tensor_scalar(sin_ar[:, t, :], sin_a[:, t, :], rstd_col[:, t:t + 1], None, ALU.mult)
                step.done(last)
                split(l, 4)
                used(l, T_Q + 1)
                rope_a(l, 0)
                rope_a(l, 1)
                split(l, 5)
                used(l, T_K + 1)
                rope_a(l, 2)
                rope_a(l, 3)
                split(l, 6)
                split(l, 7)
                split(l, 8)
                split(l, 9)
                dve.wait_ge(lat_squared, l * 4 + 4)
                dve.wait_ge(rope_sum, l * 4 + 4)
                rstd_vector(V, step, lat_rstd[:, :, :].rearrange("p t n -> p (t n)"),
                            lat_ms[:, :, :].rearrange("p t n -> p (t n)"), work).then_inc(lat_rstd_ready, 1)
                pe = z[:, :, QL + KL:LAT]
                V.tensor_tensor(temp[:, 0, 0:64].rearrange("p (t n) -> p t n", t=TT), pe, cos_b[:, :, :], ALU.mult)
                other = temp[:, 0, 64:128].rearrange("p (t n) -> p t n", t=TT)
                V.tensor_tensor(other[:, :, 0:16], pe[:, :, 16:32], sin_b[:, :, 0:16], ALU.mult)
                V.tensor_tensor(other[:, :, 16:32], pe[:, :, 0:16], sin_b[:, :, 16:32], ALU.mult).then_inc(kpe_mul, 1)
                dve.wait_ge(lat_rstd_ready, l + 1)
                for t in range(TT):
                    V.tensor_scalar(cos_br[:, t, :], cos_b[:, t, :], lat_rstd[:, t, 0:1], None, ALU.mult)
                    last = V.tensor_scalar(sin_br[:, t, :], sin_b[:, t, :], lat_rstd[:, t, 0:1], None, ALU.mult)
                step.done(last)
                dve.wait_ge(stat_done, l * 4 + 2)
                rstd_seed(V, step, mem_rstd[:, :], ps[:, 3, 0:T + TT], mem_v).then_inc(mem_seeded, 1)
                for c in range(ZC):
                    dve.wait_ge(z_hi_done, l * ZC + c + 1)
                    b = Z_BANK[c]
                    V.scalar_tensor_tensor(out=z_lo[:, c, :], in0=ps[:, b, 0:T],
                                           scalar=gain[:, G_LAT + c:G_LAT + c + 1],
                                           in1=z_hi[:, c, :].bitcast(F32), op0=ALU.mult,
                                           op1=ALU.subtract).then_inc(z_lo_done, 1)
                split(l, T_V + 3)
                split(l, T_UQ + 2)
                for i in range(2):
                    for t in range(TT):
                        dve.wait_ge(qb_copied, l * 4 + 2 * i + t + 1)
                        src = ps[:, 2 + 2 * i + t, 0:384].rearrange("p (h n) -> p h n", h=4)
                        own = temp[:, 1 + i, 256 * t:256 * t + 128].rearrange("p (h n) -> p h n", h=4)
                        other = temp[:, 1 + i, 256 * t + 128:256 * t + 256].rearrange("p (h n) -> p h n", h=4)
                        V.tensor_tensor(own, src[:, :, NOPE:DB],
                                        cos_br[:, t, :].unsqueeze(1).broadcast_to([P, 4, ROPE]), ALU.mult)
                        for j in range(2):
                            last = V.tensor_tensor(
                                other[:, :, 16 * j:16 * j + 16], src[:, :, DB - 16 - 16 * j:DB - 16 * j],
                                sin_br[:, t, 16 * j:16 * j + 16].unsqueeze(1).broadcast_to([P, 4, 16]), ALU.mult)
                        last.then_inc(qb_mul, 1)
                    if i == 0:
                        split(l, T_UQ + 3)
                used(l, T_UKV)
                for t in range(TT):
                    for i in range(2):
                        if t == 1:
                            dve.wait_ge(kb_copied, l * 4 + i + 1)
                        src = ps[:, 6 * t + i, :].rearrange("p (h n) -> p h n", h=4)
                        V.tensor_scalar(v_b[:, t, 4 * i:4 * i + 4, :], src[:, :, NOPE:NOPE + VB],
                                        lat_rstd[:, t, 1:2], None, ALU.mult).then_inc(vb_copied, 1)
                for s in range(HEADS):
                    g = s // 2
                    if s:
                        prob_copy(l, s - 1)
                    head_max(l, s)
                    if s % 2 == 0:
                        if g == 6:
                            dve.wait_ge(mem_rstd_ready, l + 1)
                        if g >= 1:
                            gate_scale(l, g - 1)
                        head_norm(l, s)
                    else:
                        if g >= 1:
                            o_pair(l, g - 1)
                        head_norm(l, s)
                        dve.wait_ge(m_hi_done, l * 8 + g + 1)
                        V.scalar_tensor_tensor(out=m_lo[:, g, :], in0=mem[:, g, :],
                                               scalar=gain[:, G_MEM + g:G_MEM + g + 1],
                                               in1=m_hi[:, g, :].bitcast(F32), op0=ALU.mult,
                                               op1=ALU.subtract).then_inc(m_lo_done, 1)
                prob_copy(l, HEADS - 1)
                gate_scale(l, 7)
                dve.wait_ge(w_lo_done, l * TILES + T_XK + 2)
                split(l, T_XK + 2)
                o_pair(l, HEADS // 2 - 1)
                dve.wait_ge(mem_rstd_ready, l + 1)
                for j in range(2):
                    used(l, T_XK + j)
                    V.tensor_tensor(xk[:, 2 * j:2 * j + 2, :], banks(2 + j), wide(mem_row[:, :], 2),
                                    ALU.mult).then_inc(xk_copied, 1)
                    split(l, T_XK + 3 + j)
                used(l, T_BRANCH)
                dve.wait_ge(gate_tanh, l * 8 + 8)
                gated(0, 6, 0)
                gated(0, 7, 1)
                split(l, T_BRANCH + 3)
                used(l, T_BRANCH + 1)
                for p in range(2):
                    step.done(gated(1, 4 + p, p))
                    merge(l, p)
                for p in range(2):
                    merge_split(l, p)
                used(l, T_BRANCH + 2)
                gated(0, 0, 2)
                gated(0, 1, 3)
                split(l, T_BRANCH + 4)
                for p in range(2, 4):
                    if p == 2:
                        dve.wait_ge(branch_half, l + 1)
                    else:
                        used(l, T_BRANCH + 3)
                    step.done(gated(1, p, p))
                    merge(l, p)
                    merge_split(l, p)
                dve.wait_ge(w_lo_done, l * TILES + T_OUT + 2)
                split(l, T_OUT + 2)
                for j, b in enumerate(((4, 5), (6, 7), (0, 1), (2, 3))):
                    used(l, T_OUT + j)
                    add_to_x(j, b, 0.5)
                    if j < 3:
                        split(l, T_OUT + 3 + j)
                    h_split(l, 1, (2 * j, 2 * j + 1), G_X, o_hi, o_lo)
                split(l, T_XQ + 2)
                dve.wait_ge(stat_done, l * 4 + 3)
                step.done(rstd_vector(V, step, rstd_col, ps[:, 0, T:T + TT], work))
                V.tensor_scalar(x_scale[:, :], rstd_col[:, :], SCALE_X, None, ALU.mult).then_inc(rstd_ready, 1)
                dve.wait_ge(rstd_ready, l * 3 + 2)
                split(l, T_XQ + 3)

                def x_norm(j):
                    dve.wait_ge(exp_done, l * ALL_HEADS + HEADS + j + 1)
                    step.done(V.reciprocal(row_inv[j][:, :], row_sum[j][:, :]))
                    for t in range(TT):
                        last = V.tensor_scalar(xp[j][:, t, :], xp[j][:, t, :], row_inv[j][:, t:t + 1], None, ALU.mult)
                    last.then_inc(prob_ready, 1)

                for j in range(HX):
                    dve.wait_ge(scored, l * ALL_HEADS + HEADS + j + 1)
                    step.done(V.tensor_reduce(row_max[j][:, :], ps[:, j, :].rearrange("p (t k) -> p t k", t=TT), AX.X,
                                              ALU.max))
                    V.scalar_tensor_tensor(out=bias[j][:, :], in0=row_max[j][:, :], scalar=-1.0, in1=x_scale[:, :],
                                           op0=ALU.mult, op1=ALU.mult).then_inc(max_ready, 1)
                x_norm(0)
                x_norm(1)
                split(l, T_XV + 2)
                x_norm(2)
                x_norm(3)
                split(l, T_XV + 3)
                for j in range(HX):
                    if j == 2:
                        used(l, T_XV + 1)
                        V.tensor_scalar(xv[:, 1, :], ps[:, 7, :], mem_col[:, 1:2], None,
                                        ALU.mult).then_inc(xv_copied, 1)
                    dve.wait_ge(prob_turned, l * ALL_HEADS + HEADS + j + 1)
                    if j >= 2:
                        dve.wait_ge(attended, l * ALL_HEADS + HEADS + j - 1)
                    V.tensor_copy(xpt[j % 2].rearrange("p a b -> p (a b)"), ps[:, j, :]).then_inc(prob_copied, 1)
                for r in range(2):
                    dve.wait_ge(o_hi_done, l * 10 + 8 + r + 1)
                    V.tensor_tensor(o_lo[:, 2 * r:2 * r + 2, :], banks(4 + r),
                                    o_hi[:, 2 * r:2 * r + 2, :].bitcast(F32), ALU.subtract).then_inc(o_lo_done, 1)
                split(l, T_XO + 2)
                used(l, T_XO)
                add_to_x(0, 6, 1.0)
                add_to_x(1, 7, 1.0)
                h_split(l, 2, range(4), G_FFN)
                dve.wait_ge(pair_done, l * 4 + 1)
                add_to_x(2, 0, 1.0)
                used(l, T_XO + 1)
                add_to_x(3, 1, 1.0)
                h_split(l, 2, range(4, DC), G_FFN)
                split(l, T_XO + 3)
                dve.wait_ge(h_lo_done, l * 24 + 24)
                V.tensor_copy(gain[:, :], gain_all[:, bass.ds(l * GAINS + GAINS, GAINS)]).then_inc(gains_ready, 1)
                split(l, T_FFN + 2)
                split(l, T_FFN + 3)
                dve.wait_ge(stat_done, l * 4 + 4)
                rstd_vector(V, step, rstd_row, ps[:, 3, 0:T], work).then_inc(rstd_ready, 1)
                dve.wait_ge(rstd_ready, l * 3 + 3)
                hidden_scale(5)
                split(l, T_FFN + 4)
                hidden_gate(l * NSLICE)
                used(l, T_FFN + 1)
                hidden_times_up(l * NSLICE, b=7)
                used(l, T_FFN + 2)
                hidden_scale(4)
                split(l, T_FFN + 5)
                hidden_gate(l * NSLICE + 1)
                split(l, T_FFN + 6)
                done = step.n
                with dve.Fori(0, LOOPS) as k:
                    def loop_split(j):
                        slot = (T_LOOP + 2 + j) % SLOTS
                        dve.wait_ge(w_hi_done, l * TILES + k * 3 + (T_LOOP + 2 + j + 1))
                        V.tensor_tensor(w_lo[slot][:, :], raw[slot][:, :], w_hi[slot][:, :].bitcast(F32),
                                        ALU.subtract).then_inc(w_lo_done, 1)
                    step.start(l * DVE_STEPS + k + (start + done))
                    dve.wait_ge(tile_used, l * TILES + k * 3 + (T_LOOP - 1 + 2))
                    hidden_times_up(l * NSLICE + k + 1)
                    loop_split(0)
                    dve.wait_ge(tile_used, l * TILES + k * 3 + (T_LOOP + 2))
                    hidden_scale(4)
                    loop_split(1)
                    hidden_gate(l * NSLICE + k + 2)
                    loop_split(2)
                assert step.n == 1 and done + LOOPS + 1 == DVE_STEPS, (step.n, done + LOOPS + 1, DVE_STEPS)
                step.start(l * DVE_STEPS + (start + done + LOOPS))
                used(l, T_END - 1)
                hidden_times_up(l * NSLICE + (NSLICE - 2))
                split(l, T_END + 2)
                used(l, T_END)
                hidden_scale(4)
                split(l, T_END + 3)
                hidden_gate(l * NSLICE + (NSLICE - 1))
                used(l, T_END + 1)
                hidden_times_up(l * NSLICE + (NSLICE - 1), a_hi_last, a_lo_last)
                split(l, TILES)
                for p in range(3):
                    dve.wait_ge(pair_done, l * 4 + 2 + p)
                    add_to_x(p, p, 0.5)
                used(l, T_LAST)
                add_to_x(3, 3, 0.5)
            dve.wait_ge(gains_ready, DEPTH + 1)
            dve.wait_ge(x_ready, (DEPTH + 1) * 12 - 8)
            for c in range(DC):
                V.tensor_scalar(x_gain[:, c, :], x[:, c, :], gain[:, c:c + 1], None, ALU.mult).then_inc(final_scaled, 1)
            step.start(DEPTH * DVE_STEPS + start)
            dve.wait_ge(final_stat, 1)
            rstd_vector(V, step, rstd_col, ps[:, 0, 0:TT], work).then_inc(final_stat, 1)
            dve.wait_ge(final_stat, 2)
            for t in range(TT):
                dve.wait_ge(final_turned, t + 1)
                V.tensor_scalar(y[:, t, 512:1024], ps[:, 5 + 2 * t, :], rstd_col[:, t:t + 1], None,
                                ALU.mult).then_inc(y_ready[1], 1)

        @block.tensor
        def _(pe):
            mm = nc.tensor.matmul

            def cut(n):
                c, m = tile_cut(n)
                hi = w_hi[n % SLOTS][:, 0:c * m].rearrange("p (c n) -> p c n", c=c)
                lo = w_lo[n % SLOTS][:, 0:c * m].rearrange("p (c n) -> p c n", c=c)
                return hi, lo

            def by_token(n, a_hi, a_lo, c0, outs, first, last):
                hi, lo = cut(n)
                chunks = tile_cut(n)[0]
                for c in range(chunks):
                    for t in range(TT):
                        ah = a_hi[:, c0 + c, t * P:t * P + P]
                        al = a_lo[:, c0 + c, t * P:t * P + P]
                        for b, col, m in outs[t]:
                            begin, end = first and c == 0, last and c == chunks - 1
                            out = ps[:, b, 0:m]
                            mm(out, ah, hi[:, c, col:col + m], start=begin, stop=False)
                            mm(out, ah, lo[:, c, col:col + m], start=False, stop=False)
                            ins = mm(out, al, hi[:, c, col:col + m], start=False, stop=end)
                return ins

            def three(out, hi, lo, c, col, ah, al, begin, end, open_bank=False):
                wh, wl = hi[:, c, col:col + P], lo[:, c, col:col + P]
                mm(out, wh, ah, start=begin, stop=False, skip_group_check=open_bank)
                mm(out, wh, al, start=False, stop=False, skip_group_check=open_bank)
                return mm(out, wl, ah, start=False, stop=end, skip_group_check=open_bank)

            def by_feature(n, a_hi, a_lo, outs, before=None, half_done=None):
                hi, lo = cut(n)
                chunks = tile_cut(n)[0]
                for j, out in enumerate(outs):
                    if before is not None:
                        before(j)
                    for c in range(chunks):
                        ins = three(out, hi, lo, c, P * j, a_hi[:, c, :], a_lo[:, c, :], c == 0, c == chunks - 1)
                    if half_done is not None and j == 1:
                        ins.then_inc(half_done, 1)
                return ins

            def as_chunks_come(n, a_hi, a_lo, outs, before):
                hi, lo = cut(n)
                for c in range(DC):
                    before(c)
                    for j, out in enumerate(outs):
                        ins = three(out, hi, lo, c, P * j, a_hi[:, c, :], a_lo[:, c, :], c == 0, c == DC - 1)
                return ins

            def halves(b):
                return [ps[:, b, 0:T], ps[:, b, T:2 * T]]

            def split_done(l, n):
                pe.wait_ge(w_lo_done, l * TILES + n + 1)

            def h_ready(l, norm, c):
                pe.wait_ge(h_lo_done, l * 24 + 8 * norm + c + 1)

            def statistics(value, b, row=True, col=True, square_sum=square_sum):
                pe.wait_ge(sums_ready, value)
                if row:
                    ins = mm(ps[:, b, 0:T], mean_of[:, :], square_sum[:, :], start=True, stop=True)
                if col:
                    for t in range(TT):
                        ins = mm(ps[:, b, T + t:T + t + 1], square_sum[:, t * P:t * P + P], mean_of[:, 0:1],
                                 start=True, stop=True)
                ins.then_inc(stat_done, 1)

            def turn_head(l, u):
                if u == 0:
                    pe.wait_ge(rope_sum, l * 4 + 4)
                    pe.wait_ge(qb_copied, l * 4 + 4)
                    pe.wait_ge(qb_mul, l * 4 + 4)
                else:
                    pe.wait_ge(head_copied, l * TURNS + u)
                if u == HA // 2:
                    pe.wait_ge(qb_sum, l * 4 + 4)
                    pe.wait_ge(kpe_sum, l + 1)
                d = P if u < HA // 2 else DB
                for i in range(4):
                    t = i % 2
                    if u < HA // 2:
                        src = (q_a, k_a)[i // 2][:, t, P * u:P * u + P]
                    else:
                        src = (q_b, k_b)[i // 2][:, t, u - HA // 2, :]
                    ins = nc.tensor.transpose(ps[0:d, 5, P * i:P * i + P], src, ident[:, :])
                ins.then_inc(head_turned, 1)

            def score(l, s):
                u = turn_of(s)
                d = slice(DA * (s % 2), DA * (s % 2) + DA) if s < HA else slice(0, DB)
                pe.wait_ge(head_copied, l * TURNS + u + 1)
                if s >= 2:
                    pe.wait_ge(exp_done, l * ALL_HEADS + s - 1)
                src, b = qk_t[u % 2], 6 + s % 2
                mm(ps[:, b, 0:P], src[d, 0:P], src[d, 2 * P:3 * P], start=True, stop=False)
                mm(ps[:, b, 0:P], ident_h[:, :], mask[:, :], start=False, stop=True)
                mm(ps[:, b, P:3 * P], src[d, P:2 * P], src[d, 2 * P:4 * P], start=True, stop=False)
                mm(ps[:, b, 2 * P:3 * P], ident_h[:, :], mask[:, :], start=False, stop=True).then_inc(scored, 1)

            def turn_prob(l, s):
                pe.wait_ge(prob_ready, l * ALL_HEADS + s + 1)
                if s:
                    pe.wait_ge(prob_copied, l * ALL_HEADS + s)
                for i in range(3):
                    ins = nc.tensor.transpose(ps[:, 4, P * i:P * i + P], prob[s % 2][:, P * i:P * i + P], ident[:, :])
                ins.then_inc(prob_turned, 1)

            def attend(l, s):
                pe.wait_ge(prob_copied, l * ALL_HEADS + s + 1)
                r = s // 2
                if r >= 2 and s % 2 == 0:
                    pe.wait_ge(o_lo_done, l * 10 + r - 1)
                part = slice(64 * (s % 2), 64 * (s % 2) + 64)
                v = [v_a[:, t, DA * s:DA * s + DA] if s < HA else v_b[:, t, s - HA, :] for t in range(TT)]
                mm(ps[part, r % 2, 0:T], v[0], prob_t[s % 2][:, 0:T], start=True, stop=False)
                mm(ps[part, r % 2, P:T], v[1], prob_t[s % 2][:, T:T + P], start=False,
                   stop=True).then_inc(attended, 1)

            pe.wait_ge(consts_made, 1)
            pe.sem_inc(tile_used, 1)
            pe.wait_ge(raw_landed[0], 16)
            with pe.Fori(0, 13) as _:
                for i in range(4):
                    mm(ps[:, 7, P * i:P * i + P], ident_h[:, :], mask[:, :], start=True, stop=True)
            with pe.Fori(0, DEPTH) as l:
                for i in range(2):
                    split_done(l, T_Q + i)
                    hi, lo = cut(T_Q + i)
                    for c in range(4):
                        h_ready(l, 0, 4 * i + c)
                        for t in range(TT):
                            ah = h_hi[:, 4 * i + c, t * P:t * P + P]
                            al = h_lo[:, 4 * i + c, t * P:t * P + P]
                            mm(ps[:, 4 + t, :], ah, hi[:, c, :], start=(i + c == 0), stop=False)
                            mm(ps[:, 4 + t, :], ah, lo[:, c, :], start=False, stop=False)
                            ins = mm(ps[:, 4 + t, :], al, hi[:, c, :], start=False, stop=(i == 1 and c == 3))
                    ins.then_inc(tile_used, 1)
                statistics(l * 4 + 1, 0)
                for i in range(2):
                    split_done(l, T_K + i)
                    by_token(T_K + i, h_hi, h_lo, 4 * i, [[(6, 0, 512)], [(7, 0, 512)]], i == 0,
                             i == 1).then_inc(tile_used, 1)
                pe.wait_ge(rstd_ready, l * 3 + 1)
                for i in range(3):
                    split_done(l, T_LAT + i)
                    by_token(T_LAT + i, h_hi, h_lo, 3 * i, [[(2 * t + j, 336 * j, 336) for j in range(2)]
                                                           for t in range(TT)], i == 0, i == 2).then_inc(tile_used, 1)
                pe.wait_ge(rope_mul, l * 4 + 2)
                for i in range(2):
                    split_done(l, T_V + i)
                    by_token(T_V + i, h_hi, h_lo, 4 * i, [[(4, 0, 512)], [(5, 0, 512)]], i == 0,
                             i == 1).then_inc(tile_used, 1)
                    if i == 0:
                        pe.wait_ge(lat_copied, l * 4 + 4)
                        statistics(l * 4 + 2, 3, square_sum=mem_sum)
                        pe.wait_ge(rope_mul, l * 4 + 4)
                        for c in range(ZC):
                            b = Z_BANK[c]
                            for t in range(TT):
                                ins = nc.tensor.transpose(ps[:, b, t * P:t * P + P],
                                                          z[:, t, c * P:c * P + P], ident[:, :])
                            ins.then_inc(z_turned, 1)
                pe.wait_ge(z_lo_done, l * ZC + ZC)
                pe.wait_ge(mem_seeded, l + 1)
                for i in range(2):
                    split_done(l, T_UQ + i)
                    if i == 1:
                        pe.wait_ge(v_copied, l * 2 + 2)
                    by_token(T_UQ + i, z_hi, z_lo, 0, [[(2 + 2 * i + t, 0, 384)] for t in range(TT)], True,
                             True).then_inc(tile_used, 1)
                split_done(l, T_UKV)
                by_token(T_UKV, z_hi, z_lo, 3, [[(6 * t + j, 512 * j, 512) for j in range(2)] for t in range(TT)],
                         True, True).then_inc(tile_used, 1)
                turn_head(l, 0)

                def gate_half(s, chunks):
                    g, j = divmod(s, 2)
                    hi, lo = cut(T_GATE + g)
                    if j == 0 and chunks[0] == 0:
                        split_done(l, T_GATE + g)
                        if g >= 2:
                            pe.wait_ge(gate_scaled, l * 8 + g - 1)
                    for c in chunks:
                        ins = three(halves(2 + g % 2)[j], hi, lo, c, P * j, h_hi[:, c, :], h_lo[:, c, :], c == 0,
                                    c == DC - 1)
                    return ins

                for s in range(HEADS):
                    g, j = divmod(s, 2)
                    ahead = 2 if s == 0 else 0
                    if s == 0:
                        gate_half(0, range(ahead))
                        pe.wait_ge(kb_copied, l * 4 + 2)
                        pe.wait_ge(vb_copied, l * 4 + 4)
                    if s == 1:
                        pe.wait_ge(kb_copied, l * 4 + 4)
                    score(l, s)
                    if s:
                        attend(l, s - 1)
                    if s + 1 < HEADS and turn_of(s + 1) != turn_of(s):
                        turn_head(l, turn_of(s + 1))
                    ins = gate_half(s, range(ahead, DC))
                    if j == 1:
                        ins.then_inc(tile_used, 1)
                    turn_prob(l, s)
                pe.wait_ge(m_lo_done, l * 8 + 8)
                for j in range(2):
                    pe.wait_ge(gate_scaled, l * 8 + 7 + j)
                    split_done(l, T_XK + j)
                    by_feature(T_XK + j, m_hi, m_lo, halves(2 + j)).then_inc(tile_used, 1)
                    if j == 0:
                        attend(l, HEADS - 1)
                for i, bank in enumerate((6, 4, 0, 2)):
                    split_done(l, T_BRANCH + i)
                    pe.wait_ge(o_lo_done, l * 10 + (4 if i == 0 else 8))
                    if i == 3:
                        pe.wait_ge(xk_copied, l * 2 + 2)
                    c0 = 4 * (i % 2)
                    by_feature(T_BRANCH + i, o_hi[:, c0:c0 + 4, :], o_lo[:, c0:c0 + 4, :],
                               halves(bank) + halves(bank + 1),
                               half_done=branch_half if i == 3 else None).then_inc(tile_used, 1)
                for j, bank in enumerate((4, 6, 0, 2)):
                    split_done(l, T_OUT + j)
                    as_chunks_come(T_OUT + j, h_hi, h_lo, [ps[:, bank, 0:T], ps[:, bank + 1, 0:T]],
                                   lambda c: pe.wait_ge(merge_lo, l * 4 + max(2, c // 2 + 1))
                                   if j == 0 and c % 2 == 0 else None).then_inc(tile_used, 1)
                for j, bank in enumerate((4, 6)):
                    split_done(l, T_XQ + j)
                    as_chunks_come(T_XQ + j, o_hi, o_lo, [ps[:, bank, 0:T], ps[:, bank + 1, 0:T]],
                                   lambda c: h_ready(l, 1, c) if j == 0 else None).then_inc(tile_used, 1)
                    if j == 0:
                        statistics(l * 4 + 3, 0, row=False)
                pe.wait_ge(rstd_ready, l * 3 + 2)
                for j in range(HX):
                    pe.wait_ge(xq_copied, l * 2 + j // 2 + 1)
                    for t in range(TT):
                        ins = mm(ps[:, j, t * T:t * T + T], xq[:, j, t * P:t * P + P], xk[:, j, :], start=True,
                                 stop=True)
                    ins.then_inc(scored, 1)
                def x_turn(j):
                    pe.wait_ge(prob_ready, l * ALL_HEADS + HEADS + j + 1)
                    for kt in range(TT):
                        for t in range(TT):
                            ins = nc.tensor.transpose(ps[:, j, kt * T + t * P:kt * T + t * P + P],
                                                      xp[j][:, t, kt * P:kt * P + P], ident[:, :])
                    ins.then_inc(prob_turned, 1)

                def x_attend(j):
                    pe.wait_ge(prob_copied, l * ALL_HEADS + HEADS + j + 1)
                    if j == 0:
                        pe.wait_ge(xv_copied, l * 2 + 2)
                    for kt in range(TT):
                        ins = mm(halves(4 + j // 2)[j % 2], xv[:, kt, j * DX:j * DX + DX], xpt[j % 2][:, kt, :],
                                 start=(kt == 0), stop=(kt == TT - 1))
                    ins.then_inc(attended, 1)

                for i in range(2):
                    split_done(l, T_XV + i)
                    by_token(T_XV + i, m_hi, m_lo, 4 * i, [[(6, 0, 512)], [(7, 0, 512)]], i == 0,
                             i == 1).then_inc(tile_used, 1)
                    x_turn(2 * i)
                    x_turn(2 * i + 1)
                for j in range(HX):
                    x_attend(j)
                split_done(l, T_XO)
                hi, lo = cut(T_XO)
                for c in range(HX):
                    pe.wait_ge(o_lo_done, l * 10 + 9 + c // 2)
                    for j, o in enumerate(halves(6) + halves(7)):
                        ins = three(o, hi, lo, c, P * j, o_hi[:, c, :], o_lo[:, c, :], c == 0 and j % 2 == 0,
                                    c == HX - 1, open_bank=True)
                ins.then_inc(tile_used, 1)
                split_done(l, T_XO + 1)
                by_feature(T_XO + 1, o_hi, o_lo, halves(0) + halves(1), half_done=pair_done).then_inc(tile_used, 1)

                def down(slot, first=False, last=False, a=(a_hi, a_lo)):
                    hi = w_hi[slot][:, :].rearrange("p (c n) -> p c n", c=2)
                    lo = w_lo[slot][:, :].rearrange("p (c n) -> p c n", c=2)
                    for m in range(DC):
                        for c in range(2):
                            ins = three(halves(m // 2)[m % 2], hi, lo, c, P * m, a[0][:, c, :], a[1][:, c, :],
                                        first and c == 0 and m % 2 == 0, last and c == 1, open_bank=True)
                        if last and m in (1, 3, 5):
                            ins.then_inc(pair_done, 1)
                    return ins

                split_done(l, T_FFN)
                hi, lo = cut(T_FFN)
                for c in range(DC):
                    h_ready(l, 2, c)
                    for j, o in enumerate(halves(5)):
                        ins = three(o, hi, lo, c, P * j, h_hi[:, c, :], h_lo[:, c, :], c + j == 0, c == DC - 1,
                                    open_bank=True)
                ins.then_inc(tile_used, 1)
                split_done(l, T_FFN + 1)
                by_feature(T_FFN + 1, h_hi, h_lo, halves(7),
                           lambda j: statistics(l * 4 + 4, 3, col=False) if j == 1 else None).then_inc(tile_used, 1)
                split_done(l, T_FFN + 2)
                by_feature(T_FFN + 2, h_hi, h_lo, halves(4)).then_inc(tile_used, 1)
                split_done(l, T_FFN + 3)
                pe.wait_ge(g_scaled, l * NSLICE + 1)
                by_feature(T_FFN + 3, h_hi, h_lo, halves(5)).then_inc(tile_used, 1)
                split_done(l, T_FFN + 4)
                pe.wait_ge(rstd_ready, l * 3 + 3)
                pe.wait_ge(a_lo_done, l * NSLICE + 1)
                down((T_FFN + 4) % SLOTS, first=True).then_inc(tile_used, 1)
                with pe.Fori(0, LOOPS) as k:
                    pe.wait_ge(w_lo_done, l * TILES + k * 3 + (T_LOOP + 1))
                    pe.wait_ge(g_scaled, l * NSLICE + k + 2)
                    by_feature(T_LOOP, h_hi, h_lo, halves(4)).then_inc(tile_used, 1)
                    pe.wait_ge(w_lo_done, l * TILES + k * 3 + (T_LOOP + 2))
                    pe.wait_ge(a_lo_done, l * NSLICE + k + 2)
                    down((T_LOOP + 1) % SLOTS).then_inc(tile_used, 1)
                    pe.wait_ge(w_lo_done, l * TILES + k * 3 + (T_LOOP + 3))
                    by_feature(T_LOOP + 2, h_hi, h_lo, halves(5)).then_inc(tile_used, 1)
                split_done(l, T_END)
                pe.wait_ge(g_scaled, l * NSLICE + NSLICE - 1)
                by_feature(T_END, h_hi, h_lo, halves(4)).then_inc(tile_used, 1)
                split_done(l, T_END + 1)
                pe.wait_ge(hidden_ready, l * NSLICE + NSLICE - 1)
                by_feature(T_END + 1, h_hi, h_lo, halves(5)).then_inc(tile_used, 1)
                split_done(l, T_END + 2)
                pe.wait_ge(a_lo_done, l * NSLICE + NSLICE - 1)
                down((T_END + 2) % SLOTS).then_inc(tile_used, 1)
                split_done(l, T_LAST)
                pe.wait_ge(a_lo_done, l * NSLICE + NSLICE)
                down(T_LAST % SLOTS, last=True, a=(a_hi_last, a_lo_last)).then_inc(tile_used, 1)
            for c in range(DC):
                pe.wait_ge(final_squared, c // 2 + 1)
                for t in range(TT):
                    ins = mm(ps[:, 0, t:t + 1], temp[:, c // 2, (c % 2) * T + t * P:(c % 2) * T + t * P + P],
                             mean_of[:, 0:1], start=(c + t == 0), stop=(c == DC - 1), skip_group_check=True)
            ins.then_inc(final_stat, 1)
            for t in range(TT):
                for c in range(DC):
                    pe.wait_ge(final_scaled, c + 1)
                    ins = nc.tensor.transpose(ps[:, 4 + 2 * t + c // 4, P * (c % 4):P * (c % 4) + P],
                                              x_gain[:, c, t * P:t * P + P], ident[:, :])
                ins.then_inc(final_turned, 1)


def kernel(**inputs):
    import concourse.bacc as bacc
    from concourse.bass_utils import run_bass_kernel_spmd

    def columns(g, chunks):
        g = np.asarray(g)
        g = g.reshape(g.shape[:-1] + (chunks, P))
        return np.moveaxis(g, -1, 0)

    per_layer = np.concatenate(
        [columns(inputs[n], c) for n, c in (("norm_mix", DC), ("norm_xattn", DC), ("norm_mem", DC), ("norm_ffn", DC),
                                            ("q_lat_norm", QL // P), ("kv_lat_norm", KL // P))], axis=2)
    gains = np.concatenate([per_layer.reshape(P, DEPTH * GAINS), columns(inputs["norm_final"], DC),
                            np.zeros((P, GAINS - DC), np.float32)], axis=1)
    freq = np.concatenate([np.exp(np.float32(-math.log(THETA) * (2.0 / d)) * np.arange(d // 2, dtype=np.float32))
                           for d in (DA, ROPE)]).astype(np.float32)
    arrays = {
        "xT": np.asarray(inputs["x"])[0].T, "memT": np.asarray(inputs["mem"])[0].T,
        "positions": np.asarray(inputs["positions"]).reshape(TT, P).T,
        "gains": np.concatenate([gains, np.tile(freq, (P, 1))], axis=1),
    }
    for n in ("w_in", "w_uq", "w_ukv", "w_branch_a", "w_branch_b", "w_out", "w_xq", "w_xkv", "w_xo", "w_gate_up",
              "w_down"):
        arrays[n] = np.asarray(inputs[n])
    arrays = {n: np.ascontiguousarray(a) for n, a in arrays.items()}
    nc = bacc.Bacc("TRN2", target_bir_lowering=False, num_devices=1)
    args = [nc.dram_tensor(n, a.shape, mybir.dt.from_np(a.dtype), kind="ExternalInput").ap()
            for n, a in arrays.items()]
    out = nc.dram_tensor("out", (T, D), F32, kind="ExternalOutput").ap()
    trunk(nc, *args, out)
    r = run_bass_kernel_spmd(nc, [arrays], core_ids=[0])
    return r.results[0]["out"][None]
```
